# Optimizing a Trainium2 kernel written in Bass

```python
import jax, jax.numpy as jnp
from jax import lax
import numpy as np

D_MODEL = 1024
BATCH = 1
SEQ = 512
DEPTH = 1

HEAD_DIM = 64
N_HEADS_NSA = 8
N_KV_NSA = 2
GROUP_NSA = N_HEADS_NSA // N_KV_NSA
N_HEADS_DIL = 8
ROPE_THETA = 500000.0
ROPE_DIM = HEAD_DIM // 4
CMP_BLOCK = 32
CMP_STRIDE = 16
CMP_HIDDEN = 256
SLC_BLOCK = 64
SLC_TOPK = 16
WIN_NSA = 512
DIL_CONFIGS = ((128, 1), (512, 4), (2048, 16))
BAND_BLOCK = 128
SLC_CHUNK = 64
N_EXPERTS = 32
TOP_K = 4
D_FF = D_MODEL
SWIGLU_LIMIT = 7.0
SWIGLU_ALPHA = 1.702
RMS_EPS = 1e-6
NEG_INF = -1e30
FORCE_SCORE = 1e9

Q_NSA = N_HEADS_NSA * HEAD_DIM
KV_NSA = N_KV_NSA * HEAD_DIM
Q_DIL = N_HEADS_DIL * HEAD_DIM
MIX_WIDTH = Q_NSA + Q_DIL
IN_WIDTHS = (Q_NSA, KV_NSA, KV_NSA, KV_NSA, KV_NSA, KV_NSA, KV_NSA, 3 * N_HEADS_NSA, Q_DIL, Q_DIL, Q_DIL)
IN_WIDTH = sum(IN_WIDTHS)
IN_SPLITS = tuple(int(s) for s in np.cumsum(IN_WIDTHS)[:-1])
SCALE = HEAD_DIM ** -0.5

kernel_name = "hybrid_nsa_dilated_moe_layer"

def rms_norm(x, g):
    xf = x.astype(jnp.float32)
    y = xf * lax.rsqrt(jnp.mean(xf * xf, axis=-1, keepdims=True) + RMS_EPS)
    return (y * g.astype(jnp.float32)).astype(x.dtype)

def rope_partial(x, positions):
    half = ROPE_DIM // 2
    inv = ROPE_THETA ** (-jnp.arange(half, dtype=jnp.float32) / half)
    ang = positions.astype(jnp.float32)[..., None] * inv
    cos = jnp.cos(ang)[:, :, None, :]
    sin = jnp.sin(ang)[:, :, None, :]
    xr = x[..., :ROPE_DIM].astype(jnp.float32)
    x1, x2 = xr[..., :half], xr[..., half:]
    rot = jnp.concatenate([x1 * cos - x2 * sin, x2 * cos + x1 * sin], axis=-1).astype(x.dtype)
    return jnp.concatenate([rot, x[..., ROPE_DIM:]], axis=-1)

def band_attention(q, k, v, max_dist):
    B, Hk, R, L, hd = q.shape
    blk = BAND_BLOCK
    n_prev = -(-max_dist // blk)
    nb = -(-L // blk)
    pad = nb * blk - L
    qb = jnp.pad(q, ((0, 0), (0, 0), (0, 0), (0, pad), (0, 0))).reshape(B, Hk, R, nb, blk, hd)
    kv_pad = ((0, 0), (0, 0), (n_prev * blk, pad), (0, 0))
    kb = jnp.pad(k, kv_pad).reshape(B, Hk, nb + n_prev, blk, hd)
    vb = jnp.pad(v, kv_pad).reshape(B, Hk, nb + n_prev, blk, hd)
    kseg = jnp.concatenate([kb[:, :, i:i + nb] for i in range(n_prev + 1)], axis=3)
    vseg = jnp.concatenate([vb[:, :, i:i + nb] for i in range(n_prev + 1)], axis=3)
    s = jnp.einsum("bhrnqd,bhnkd->bhrnqk", qb, kseg, preferred_element_type=jnp.float32) * SCALE
    start = jnp.arange(nb)[:, None, None] * blk
    qpos = start + jnp.arange(blk)[None, :, None]
    kpos = start - n_prev * blk + jnp.arange((n_prev + 1) * blk)[None, None, :]
    dist = qpos - kpos
    mask = (dist >= 0) & (dist <= max_dist) & (kpos >= 0)
    s = jnp.where(mask, s, NEG_INF)
    lse = jax.nn.logsumexp(s, axis=-1, keepdims=True)
    p = jnp.exp(s - lse).astype(v.dtype)
    o = jnp.einsum("bhrnqk,bhnkd->bhrnqd", p, vseg).reshape(B, Hk, R, nb * blk, hd)[:, :, :, :L]
    lse = lse.reshape(B, Hk, R, nb * blk)[:, :, :, :L]
    return o, lse

def dilated_attention(q, k, v):
    B, S, H, hd = q.shape
    outs, lses = [], []
    for window, dil in DIL_CONFIGS:
        m = S // dil

        def split(t):
            return t.reshape(B, m, dil, H, hd).transpose(0, 3, 2, 1, 4).reshape(B, H * dil, m, hd)

        o, lse = band_attention(split(q)[:, :, None], split(k), split(v), window // dil)
        outs.append(o[:, :, 0].reshape(B, H, dil, m, hd).transpose(0, 3, 2, 1, 4).reshape(B, S, H, hd))
        lses.append(lse[:, :, 0].reshape(B, H, dil, m).transpose(0, 3, 2, 1).reshape(B, S, H))
    w = jax.nn.softmax(jnp.stack(lses, axis=0), axis=0)
    return jnp.einsum("cbsh,cbshd->bshd", w.astype(q.dtype), jnp.stack(outs, axis=0))

def nsa_attention(q, k_cmp, v_cmp, k_slc, v_slc, k_win, v_win, gates, positions,
                  cmp_pos, w_ck1, w_ck2, w_cv1, w_cv2):
    B, S, Hq, hd = q.shape
    Hk, R = N_KV_NSA, GROUP_NSA
    t = jnp.arange(S)

    def heads_q(a):
        return a.reshape(B, S, Hk, R, hd).transpose(0, 2, 3, 1, 4)

    def heads_kv(a):
        return a.transpose(0, 2, 1, 3)

    n16 = S // CMP_STRIDE
    n_cmp = n16 - 1

    def compress(a, w1, w2):
        seg = heads_kv(a).reshape(B, Hk, n16, CMP_STRIDE, hd)
        blocks = jnp.concatenate([seg[:, :, :-1], seg[:, :, 1:]], axis=3) + cmp_pos
        hid = jax.nn.gelu(blocks.reshape(B, Hk, n_cmp, CMP_BLOCK * hd) @ w1)
        return hid @ w2

    kc = compress(k_cmp, w_ck1, w_ck2)
    vc = compress(v_cmp, w_cv1, w_cv2)
    q_raw = heads_q(q)
    s_c = jnp.einsum("bhrqd,bhcd->bhrqc", q_raw, kc, preferred_element_type=jnp.float32) * SCALE
    c_idx = jnp.arange(n_cmp)
    valid_c = (c_idx[None, :] * CMP_STRIDE + CMP_BLOCK - 1) <= t[:, None]
    p_c = jax.nn.softmax(jnp.where(valid_c, s_c, NEG_INF), axis=-1) * valid_c
    o_cmp = jnp.einsum("bhrqc,bhcd->bhrqd", p_c.astype(vc.dtype), vc)

    n_slc = S // SLC_BLOCK
    j_idx = jnp.arange(n_slc)
    cs = c_idx * CMP_STRIDE
    js = j_idx * SLC_BLOCK
    ov = jnp.clip(jnp.minimum(cs[:, None] + CMP_BLOCK, js[None, :] + SLC_BLOCK)
                  - jnp.maximum(cs[:, None], js[None, :]), 0, None).astype(jnp.float32) / CMP_BLOCK
    p_slc = jnp.einsum("bhqc,cj->bhqj", p_c.sum(axis=2), ov)
    cur = t // SLC_BLOCK
    valid_s = j_idx[None, :] <= cur[:, None]
    forced = (j_idx[None, :] == 0) | (j_idx[None, :] == cur[:, None]) | (j_idx[None, :] == cur[:, None] - 1)
    score = jnp.where(forced, FORCE_SCORE, jnp.where(valid_s, p_slc, -1.0))
    k_sel = min(SLC_TOPK, n_slc)
    _, sel = lax.top_k(score, k_sel)

    q_rot = heads_q(rope_partial(q, positions))
    kb = heads_kv(rope_partial(k_slc, positions)).reshape(B, Hk, n_slc, SLC_BLOCK, hd)
    vb = heads_kv(v_slc).reshape(B, Hk, n_slc, SLC_BLOCK, hd)
    nc = S // SLC_CHUNK
    q_chunks = q_rot.reshape(B, Hk, R, nc, SLC_CHUNK, hd).transpose(3, 0, 1, 2, 4, 5)
    sel_chunks = sel.reshape(B, Hk, nc, SLC_CHUNK, k_sel).transpose(2, 0, 1, 3, 4)
    t_chunks = t.reshape(nc, SLC_CHUNK)

    def one_chunk(args):
        qc, ic, tc = args
        flat = ic.reshape(B, Hk, SLC_CHUNK * k_sel)[..., None, None]
        kg = jnp.take_along_axis(kb, flat, axis=2).reshape(B, Hk, SLC_CHUNK, k_sel * SLC_BLOCK, hd)
        vg = jnp.take_along_axis(vb, flat, axis=2).reshape(B, Hk, SLC_CHUNK, k_sel * SLC_BLOCK, hd)
        kpos = (ic[..., None] * SLC_BLOCK + jnp.arange(SLC_BLOCK)).reshape(B, Hk, SLC_CHUNK, k_sel * SLC_BLOCK)
        s = jnp.einsum("bhrcd,bhckd->bhrck", qc, kg, preferred_element_type=jnp.float32) * SCALE
        mask = (kpos <= tc[:, None])[:, :, None]
        p = jax.nn.softmax(jnp.where(mask, s, NEG_INF), axis=-1)
        return jnp.einsum("bhrck,bhckd->bhrcd", p.astype(vg.dtype), vg)

    o_slc = lax.map(one_chunk, (q_chunks, sel_chunks, t_chunks))
    o_slc = o_slc.transpose(1, 2, 3, 0, 4, 5).reshape(B, Hk, R, S, hd)

    o_win, _ = band_attention(q_rot, heads_kv(rope_partial(k_win, positions)), heads_kv(v_win), WIN_NSA - 1)

    g = jax.nn.sigmoid(gates.reshape(B, S, Hk, R, 3).transpose(0, 2, 3, 1, 4))
    o = g[..., 0:1] * o_cmp + g[..., 1:2] * o_slc + g[..., 2:3] * o_win
    return o.transpose(0, 3, 1, 2, 4).reshape(B, S, Q_NSA)

def mixing(h, positions, w_in, cmp_pos, w_ck1, w_ck2, w_cv1, w_cv2, g_out_nsa, g_out_dil, w_o):
    B, S, _ = h.shape
    proj = h @ w_in
    q_a, kc, vc, ks, vs, kw, vw, gts, q_b, k_b, v_b = jnp.split(proj, IN_SPLITS, axis=-1)
    kvh = lambda a: a.reshape(B, S, N_KV_NSA, HEAD_DIM)
    o_a = nsa_attention(q_a.reshape(B, S, N_HEADS_NSA, HEAD_DIM), kvh(kc), kvh(vc), kvh(ks), kvh(vs),
                        kvh(kw), kvh(vw), gts.reshape(B, S, N_HEADS_NSA, 3), positions,
                        cmp_pos, w_ck1, w_ck2, w_cv1, w_cv2)
    dh = lambda a: a.reshape(B, S, N_HEADS_DIL, HEAD_DIM)
    o_b = dilated_attention(rope_partial(dh(q_b), positions), rope_partial(dh(k_b), positions), dh(v_b))
    o_b = o_b.reshape(B, S, Q_DIL)
    y = jnp.concatenate([rms_norm(o_a, g_out_nsa), rms_norm(o_b, g_out_dil)], axis=-1)
    return y @ w_o

def clamped_swiglu(u):
    x_glu, x_lin = u[..., ::2], u[..., 1::2]
    x_glu = jnp.minimum(x_glu, SWIGLU_LIMIT)
    x_lin = jnp.clip(x_lin, -SWIGLU_LIMIT, SWIGLU_LIMIT)
    return x_glu * jax.nn.sigmoid(SWIGLU_ALPHA * x_glu) * (x_lin + 1)

def moe(h, w_router, b_router, w_up, b_up, w_down, b_down):
    B, S, D = h.shape
    hf = h.reshape(B * S, D)
    logits = (hf @ w_router + b_router).astype(jnp.float32)
    top_val, top_idx = lax.top_k(logits, TOP_K)
    gate = jax.nn.softmax(top_val, axis=-1)
    flat_e = top_idx.reshape(-1)
    order = jnp.argsort(flat_e)
    e_sorted = flat_e[order]
    tok = order // TOP_K
    g_sorted = gate.reshape(-1)[order]
    group_sizes = jnp.zeros((N_EXPERTS,), jnp.int32).at[flat_e].add(1)
    xs = hf[tok]
    up = lax.ragged_dot(xs, w_up, group_sizes) + b_up[e_sorted]
    down = lax.ragged_dot(clamped_swiglu(up), w_down, group_sizes) + b_down[e_sorted]
    out = jnp.zeros_like(hf).at[tok].add(down * g_sorted[:, None].astype(down.dtype))
    return out.reshape(B, S, D)

def setup_inputs(seed: int = 0) -> dict:
    key = jax.random.key(seed)
    ks = jax.random.split(key, 26)
    f32 = jnp.float32
    L = DEPTH

    def nrm(k, shape, scale):
        return jax.random.normal(k, shape, f32) * scale

    def gain(k, shape):
        return 1.0 + 0.05 * jax.random.normal(k, shape, f32)

    start = jax.random.randint(ks[2], (BATCH, 1), 0, 2048, jnp.int32)
    return {
        "x": nrm(ks[0], (BATCH, SEQ, D_MODEL), 1.0),
        "c": nrm(ks[1], (BATCH, D_MODEL), 1.0),
        "positions": start + jnp.arange(SEQ, dtype=jnp.int32)[None, :],
        "w_ada": nrm(ks[3], (L, D_MODEL, 6 * D_MODEL), D_MODEL ** -0.5),
        "b_ada": nrm(ks[4], (L, 6 * D_MODEL), 0.02),
        "g_pre_mix": gain(ks[5], (L, D_MODEL)),
        "g_post_mix": gain(ks[6], (L, D_MODEL)),
        "g_pre_ffn": gain(ks[7], (L, D_MODEL)),
        "g_post_ffn": gain(ks[8], (L, D_MODEL)),
        "w_in": nrm(ks[9], (L, D_MODEL, IN_WIDTH), D_MODEL ** -0.5),
        "cmp_pos": nrm(ks[10], (L, CMP_BLOCK, HEAD_DIM), 0.1),
        "w_cmp_k1": nrm(ks[11], (L, CMP_BLOCK * HEAD_DIM, CMP_HIDDEN), (CMP_BLOCK * HEAD_DIM) ** -0.5),
        "w_cmp_k2": nrm(ks[12], (L, CMP_HIDDEN, HEAD_DIM), CMP_HIDDEN ** -0.5),
        "w_cmp_v1": nrm(ks[13], (L, CMP_BLOCK * HEAD_DIM, CMP_HIDDEN), (CMP_BLOCK * HEAD_DIM) ** -0.5),
        "w_cmp_v2": nrm(ks[14], (L, CMP_HIDDEN, HEAD_DIM), CMP_HIDDEN ** -0.5),
        "g_out_nsa": gain(ks[15], (L, Q_NSA)),
        "g_out_dil": gain(ks[16], (L, Q_DIL)),
        "w_o": nrm(ks[17], (L, MIX_WIDTH, D_MODEL), MIX_WIDTH ** -0.5),
        "w_router": nrm(ks[18], (L, D_MODEL, N_EXPERTS), D_MODEL ** -0.5),
        "b_router": nrm(ks[19], (L, N_EXPERTS), 0.01),
        "w_up": nrm(ks[20], (L, N_EXPERTS, D_MODEL, 2 * D_FF), D_MODEL ** -0.5),
        "b_up": nrm(ks[21], (L, N_EXPERTS, 2 * D_FF), 0.02),
        "w_down": nrm(ks[22], (L, N_EXPERTS, D_FF, D_MODEL), D_FF ** -0.5),
        "b_down": nrm(ks[23], (L, N_EXPERTS, D_MODEL), 0.02),
    }

def reference(x, c, positions, w_ada, b_ada, g_pre_mix, g_post_mix, g_pre_ffn, g_post_ffn,
              w_in, cmp_pos, w_cmp_k1, w_cmp_k2, w_cmp_v1, w_cmp_v2, g_out_nsa, g_out_dil, w_o,
              w_router, b_router, w_up, b_up, w_down, b_down):
    for l in range(DEPTH):
        mod = jax.nn.silu(c) @ w_ada[l] + b_ada[l]
        sh_m, sc_m, gt_m, sh_f, sc_f, gt_f = [m[:, None, :] for m in jnp.split(mod, 6, axis=-1)]
        h = rms_norm(x, g_pre_mix[l]) * (1 + sc_m) + sh_m
        y = mixing(h, positions, w_in[l], cmp_pos[l], w_cmp_k1[l], w_cmp_k2[l], w_cmp_v1[l], w_cmp_v2[l],
                   g_out_nsa[l], g_out_dil[l], w_o[l])
        x = x + gt_m * rms_norm(y, g_post_mix[l])
        h = rms_norm(x, g_pre_ffn[l]) * (1 + sc_f) + sh_f
        y = moe(h, w_router[l], b_router[l], w_up[l], b_up[l], w_down[l], b_down[l])
        x = x + gt_f * rms_norm(y, g_post_ffn[l])
    return x


_drawn_inputs = setup_inputs


def setup_inputs(seed=0):
    import zlib

    import numpy as np

    out = dict(_drawn_inputs(seed))
    spreads = {}
    factors = {'b_up': 6.024, 'b_down': 8.0}
    for name, (base, spread) in spreads.items():
        noise = np.random.default_rng([zlib.crc32(name.encode()), seed]).standard_normal(out[name].shape)
        drawn = base * np.exp(spread * noise) if base else spread * noise
        out[name] = __import__('jax').numpy.asarray(drawn.astype(out[name].dtype))
    for name, factor in factors.items():
        out[name] = (out[name] * factor).astype(out[name].dtype)
    return out
```

```python
from contextlib import ExitStack

import numpy as np

import concourse.bass as bass
from concourse import mybir

ALU = mybir.AluOpType
ACT = mybir.ActivationFunctionType
AX = mybir.AxisListType
F32 = mybir.dt.float32
BF16 = mybir.dt.bfloat16
I32 = mybir.dt.int32
U32 = mybir.dt.uint32

P = 128
SEQ = 512
D = 1024
NT = SEQ // P
KT = D // P
HD = 64
N_EXP = 32
TOP_K = 4
DFF = 1024
EPS = 1e-6
NEG = -1e30
SLOTS = 64
LIMIT = 7.0
ALPHA = 1.702
N_SLC, N_WIN, N_DIL = 0, 1, 2
MAGIC = 12582912.0
PAD_ROW = 1024

C_ID, C_IOTA, C_TRI, C_MB, C_MULT, C_CM, C_CV, C_US = 0, 128, 256, 384, 896, 1408, 1536, 1664
C_INVF, C_SEL4, C_RT, C_HALF, C_PADH, C_NEGP, C_I32 = 1792, 1800, 1801, 1849, 1850, 1851, 1852
C_ALL = 1884


def shape_constants():
    t = np.zeros((P, C_ALL), np.float32)
    p = np.arange(P)
    q = np.arange(P)
    t[:, C_ID:C_ID + P] = np.eye(P)
    t[:, C_IOTA:C_IOTA + P] = (q % SLOTS)[None]
    t[:, C_TRI:C_TRI + P] = np.where(q[None] <= p[:, None], 0.0, NEG)
    for blk in range(NT):
        dist = (NT - 1 - blk) * P + p[:, None] - q[None]
        mult = (dist >= 0) * ((dist <= 128).astype(int) + (dist % 4 == 0) + (dist % 16 == 0))
        t[:, C_MULT + blk * P:C_MULT + (blk + 1) * P] = mult
        t[:, C_MB + blk * P:C_MB + (blk + 1) * P] = np.where(mult > 0, 0.0, NEG)
    for i in range(NT):
        c = np.arange(32)
        ok = (c[None] * 16 + 31 <= (i * P + p)[:, None]) & (c[None] < 31)
        t[:, C_CV + 32 * i:C_CV + 32 * (i + 1)] = ok
        t[:, C_CM + 32 * i:C_CM + 32 * (i + 1)] = np.where(ok, 0.0, NEG)
    t[:, C_US:C_US + P] = p[:, None] < q[None]
    t[:, C_INVF:C_INVF + 8] = (np.float32(500000.0) ** (-np.arange(8, dtype=np.float32) / np.float32(8)))[None]
    t[::32, C_SEL4] = 1.0
    for i in range(NT):
        for k in range(TOP_K):
            c = C_RT + 3 * (i * TOP_K + k)
            t[:, c], t[:, c + 1], t[:, c + 2] = p, P * i, 1.0
    half = p // SLOTS
    t[:, C_HALF] = half
    t[:, C_PADH] = half + PAD_ROW + p
    t[:, C_NEGP] = -(PAD_ROW + p)
    t[:, C_I32:C_I32 + 32] = np.arange(32)[None]
    return t


def hybrid_layer(nc, a, out):
    x_d, c_d, pos_d = a["x"][0], a["c"], a["positions"]
    w_ada = a["w_ada"][0].rearrange("(p j) n -> p j n", j=KT)
    w_in = a["w_in"][0].rearrange("(kt p) n -> p kt n", p=P)
    w_o = a["w_o"][0].rearrange("(kt p) n -> p kt n", p=P)
    w_c1 = [a[n][0].rearrange("(m p) n -> p m n", p=P) for n in ("w_cmp_k1", "w_cmp_v1")]
    w_up = a["w_up"][0].rearrange("e (kt p) (h y c) -> y p e kt h c", p=P, h=2, y=2)
    w_dn = a["w_down"][0].rearrange("e (h y q p) n -> y p e h q n", p=P, q=2, y=2)
    consts = nc.inline_tensor(shape_constants(), name="shape_table").ap()

    xn2_d = nc.dram_tensor("xn2_rows", (2 * SEQ, D // 2), F32).ap()
    x2_d = nc.dram_tensor("x2_rows", (SEQ, D), F32).ap()
    moe_d = nc.dram_tensor("moe_rows", (2 * SEQ + 2 * P, D // 2), F32).ap()
    bias_d = nc.dram_tensor("bias_parts", (N_EXP, 3, 3 * D), BF16).ap()

    with ExitStack() as ctx:
        W_ALL = 53200
        arena = ctx.enter_context(nc.sbuf_tensor("arena", [P, W_ALL], F32))
        ps = ctx.enter_context(nc.psum_tensor("ps", [P, 8, 512], F32))

        def sem(name):
            return ctx.enter_context(nc.semaphore(name))

        def take(at, *shape, parts=P, dt=F32):
            n = int(np.prod(shape))
            v = arena[0:parts, at:at + (n if dt in (F32, I32, U32) else n // 2)]
            if dt != F32:
                v = v.bitcast(dt)
            if len(shape) > 1:
                names = "abcd"[:len(shape)]
                v = v.rearrange(f"p ({' '.join(names)}) -> p {' '.join(names)}",
                                **{k: s for k, s in zip(names[1:], shape[1:])})
            return v

        def bc(ap, axis, n):
            v = ap.unsqueeze(axis)
            shape = list(v.shape)
            shape[axis] = n
            return v.broadcast_to(shape)

        A_AT, B_AT, D_AT, P_AT = [0, 16384], [8192, 24576], 32768, 40960
        upw = [[take(at[par], KT, 2, 512) for at in (A_AT, B_AT)] for par in range(2)]
        dnw = take(D_AT, 2, 2, 2, D)
        stage = [take(0, NT, 512), take(2048, NT, 512)]
        xn = take(0, NT, D)
        kdup = take(4096, NT, 6, 2, HD)
        ring = [take(8192, 4096), take(12288, 4096)]
        qraw, qrot, qdil, kdil = [take(16384 + 2048 * n, 4, SEQ) for n in range(4)]
        kslc, kwin = take(24576, 2, SEQ), take(25600, 2, SEQ)
        o_all = take(26624, NT, D)
        kc = take(26624, 4, SEQ)
        blk = take(30720, 16, 4, 32)
        hT = take(32768, KT, SEQ)
        xs = take(36864, NT, D)
        gel_u, gel_t, gel_e = take(0, 256), take(256, 256), take(512, 256)
        hidT, hidv = take(768, 2, P), take(1024, 2, 2, 4, 32)
        p_cmp = take(2048, NT, 256)
        pcT = take(3072, 2, NT, P)
        w2k, w2v = take(7168, 2, 2, HD), take(7424, 2, HD)
        bias_f = take(4096, 3 * D, parts=32)
        bias_b = take(26624, 3, 3 * D, parts=32, dt=BF16)

        cur = [P_AT]

        def put(*shape, parts=P, dt=F32):
            n = int(np.prod(shape))
            v = take(cur[0], *shape, parts=parts, dt=dt)
            cur[0] += n if dt in (F32, I32, U32) else (n + 1) // 2
            return v

        cf = put(C_ALL)
        ident = cf[:, C_ID:C_ID + P]
        identb, trib, usb, onesb = [put(P, dt=BF16) for _ in range(4)]
        mb_b = put(512, dt=BF16)
        cm_b = put(P, dt=BF16)
        ab2 = put(16)
        gbf = put(D)
        ctab = put(66, parts=1, dt=I32)
        fin = put(16)
        small_end = cur[0]
        sel = put(16, P, dt=BF16)
        xg = put(512)
        xgT = put(KT, SLOTS)
        sw_g, sw_s = put(2, 256), put(2, 256)
        sw_l, sw_t = put(256), put(256)
        act = put(2, 256)
        actT = put(2, 2, P)
        ybuf = put(512)
        biasw = put(2, 3 * D, parts=3, dt=BF16)
        rt = put(16, 6, dt=BF16)
        flatk = put(16)
        mraw, mt = put(6), put(8)
        idxg = put(1, dt=I32)
        gate_all, row_all = put(68), put(68)
        xg_in = cf[:, C_MB:C_MB + 512]
        gate_c, idxs_c = put(1), put(1, dt=I32)
        assert cur[0] <= W_ALL, cur[0]
        cur[0] = small_end
        v_slc, v_win, v_dil = put(NT, P), put(NT, P), put(NT, 512)
        pbuf = put(4, 512)
        ptb = put(3, 512)
        negm, lsum, osc = put(96), put(24, 4), put(2, 2, 4)
        otmp = put(2, 4, HD)
        sg = put(NT, 24)
        vt, modc, posT = put(88), put(48), put(16)
        ab1 = put(16)
        cvec, ctmp = put(KT), put(3, KT)
        posi, posf = put(NT, dt=I32), put(NT)
        ang, trig, rk = put(NT, 8), put(2, NT, 8), put(2, NT, 8)
        brow = put(32)
        st = put(6, 8)
        kcT, vc4 = put(2, 32), put(2, HD)
        sc8 = put(3, 4, 8)
        wr, ones_f = put(KT, 32), put(P)
        assert cur[0] <= W_ALL - 1, cur[0]
        gbm = ptb[:, 0:2, :].rearrange("p a b -> p (a b)")
        vr = pbuf[0:88, 0, 0:P]
        cposr = pbuf[0:16, 1, 0:P]
        mrow = pbuf[:, 2:4, :]
        rope_t = ptb[:, 0:2, :].rearrange("p a (b c) -> p (a b) c", c=256)
        silu_c = ptb[:, 2, 0:KT * 32].rearrange("p (j n) -> p j n", n=32)
        zero = pbuf[:, 3, :]
        diag = pbuf[:, 0, :].rearrange("p (a b) -> p a b", b=P)
        lg = take(16384, NT, 32)
        top8, idx8 = take(16512, NT, 8), take(16544, NT, 8, dt=U32)
        eidx = take(16576, NT, TOP_K)
        onehot = take(16640, 16, 32)
        maskb = take(17152, NT, 32, dt=BF16)
        cnt, nch = take(17216, 32), take(17248, 32)
        scan = [take(17280, 48), take(17344, 48)]
        flat_e = take(17408, NT, 32)
        prod = take(17664, 16, 32)
        gk, gres = take(18176, NT, TOP_K), take(18192, NT, TOP_K)
        gsum = take(18208, NT)
        ghi = take(18216, 3, 16, dt=BF16)
        xn2 = o_all
        yfin, x2fin = take(0, NT, D), take(4096, NT, D)

        RING = [("ada", n) for n in range(4)] + [("in", n) for n in range(6)] + [("c1", 0), ("c1", 1)] + \
               [("ada", n) for n in range(4, 12)] + [("wo", 0), ("wo", 1)]
        at_ring = {item: n for n, item in enumerate(RING)}
        IN_COLS = [(0, 512), (512, 1024), (1024, 1304), (1304, 1816), (1816, 2328), (2328, 2840)]

        def ring_view(n):
            kind, m = RING[n]
            v = ring[n % 2]
            if kind == "c1":
                return v.rearrange("p (m n) -> p m n", n=256)
            w = IN_COLS[m][1] - IN_COLS[m][0] if kind == "in" else 512
            return v[:, 0:KT * w].rearrange("p (k n) -> p k n", n=w)

        heads = [(ty, h) for ty in range(3) for h in range(8)]
        UNITS = 4 * len(heads)
        DIL_U = 4 * 16

        consts_in, x_in, vec_in, c_in, pos_in, brow_in, w2_in, bias_in, wr_in = [
            sem(n) for n in ("consts_in", "x_in", "vec_in", "c_in", "pos_in", "brow_in", "w2_in", "bias_in", "wr_in")]
        ring_in = [sem("ring_in0"), sem("ring_in1")]
        ada_ps, o_scaled, gb_sb, routed = [sem(n) for n in ("ada_ps", "o_scaled", "gb_sb", "routed")]
        row_turn = sem("row_turn")
        bconst, zeroed, bias_split, bias_out = [
            sem(n) for n in ("bconst", "zeroed", "bias_split", "bias_out")]
        vt_ps, vt_sb, row_sb, modc_ps, modc_sb = [sem(n) for n in ("vt_ps", "vt_sb", "row_sb", "modc_ps", "modc_sb")]
        chain, achain, pchain = sem("dve_chain"), sem("act_chain"), sem("pool_chain")
        silu_e, silu_ready, trig_in, trig_ready = [sem(n) for n in ("silu_e", "silu_ready", "trig_in", "trig_ready")]
        sumsq, ms_ready, root_ready = [sem(n) for n in ("sumsq", "ms_ready", "root_ready")]
        xn_ready, tile_tr, ev_dve, ev_act = [sem(n) for n in ("xn_ready", "tile_tr", "ev_dve", "ev_act")]
        pj_ps, pj_ev, roped, tg_ps, tg_ev, ab_ready = [
            sem(n) for n in ("pj_ps", "pj_ev", "roped", "tg_ps", "tg_ev", "ab_ready")]
        gate_e, blk_ready, blk_zero, hid_u, gel_in, gel_out, hid_ready, hid_tr, hid_sb, cv_ps, cv_sb = [
            sem(n) for n in ("gate_e", "blk_ready", "blk_zero", "hid_u", "gel_in", "gel_out", "hid_ready", "hid_tr",
                             "hid_sb", "cv_ps", "cv_sb")]
        sc_ps, sc_in, sc_exp, pc_ready, pc_tr, pc_sb, oc_ps, oc_sb = [
            sem(n) for n in ("sc_ps", "sc_in", "sc_exp", "pc_ready", "pc_tr", "pc_sb", "oc_ps", "oc_sb")]
        qk_done, neg_ready, exp_done, mul_done, tr_done, pt_dve, pt_act, pv_done, o_ev, o_add = [
            sem(n) for n in ("qk_done", "neg_ready", "exp_done", "mul_done", "tr_done", "pt_dve", "pt_act", "pv_done",
                             "o_ev", "o_add")]
        diag_ready, diag_ps, wo_ps, x2_ready, x2_out, xn2_out, logit_ps, mask_ready, count_ps, ctab_ready = [
            sem(n) for n in ("diag_ready", "diag_ps", "wo_ps", "x2_ready", "x2_out", "xn2_out", "logit_ps",
                             "mask_ready", "count_ps", "ctab_ready")]
        gx_in, gx_out = sem("gx_in"), sem("gx_out")
        a_in, b_in = [sem("a_in0"), sem("a_in1")], [sem("b_in0"), sem("b_in1")]
        d_in = [sem("d_in0"), sem("d_in1")]
        biasw_in = [sem("biasw_in0"), sem("biasw_in1")]
        sel_ready, sel_ps, idx_ready, gathered, moved, xg_tr, xgT_ready = [
            sem(n) for n in ("sel_ready", "sel_ps", "idx_ready", "gathered", "moved", "xg_tr", "xgT_ready")]
        up_a, up_b, glu_ready, sig_ready, act_ready, act_tr, actT_ready, dn_a, dn_b, y_ready, scattered, turn = [
            sem(n) for n in ("up_a", "up_b", "glu_ready", "sig_ready", "act_ready", "act_tr", "actT_ready", "dn_a", "dn_b",
                             "y_ready", "scattered", "pool_turn")]
        fin_in, fin_ready, out_done, tail_chain = [sem(n) for n in ("fin_in", "fin_ready", "out_done", "tail_chain")]

        PJ = {n: NT * n for n in range(6)}
        GROUPS = [("qraw", j) for j in range(4)] + [("qrot", j) for j in range(4)] + \
                 [("dup", j) for j in range(6)] + [("kwin", j) for j in range(2)] + \
                 [("qdil", j) for j in range(4)] + [("kdil", j) for j in range(4)]
        at_group = {g: n for n, g in enumerate(GROUPS)}
        NORM_X, NORM_O, NORM_Y, NORM_H, NORM_F = range(5)
        SQ_BEFORE = [0, 4, 12, 20, 24]
        TILE_H, TILE_Y, TILE_2 = 0, 8, 16

        block = ctx.enter_context(nc.Block())

        @block.sync
        def _(sp):
            sp.dma_start(cf[:, :], consts[:, :]).then_inc(consts_in, 16)
            sp.dma_start(cvec[:, :], c_d.rearrange("a (p j) -> (a p) j", j=KT)).then_inc(c_in, 16)
            vecs = [("b_ada", 48), ("g_pre_mix", 8), ("g_post_mix", 8), ("g_pre_ffn", 8), ("g_post_ffn", 8),
                    ("g_out_nsa", 4), ("g_out_dil", 4)]
            row = 0
            for name, n in vecs:
                sp.dma_start(vr[row:row + n, :], a[name].rearrange("l (r q) -> (l r) q", q=P)).then_inc(vec_in, 16)
                row += n
            sp.dma_start(cposr, a["cmp_pos"][0].rearrange("(m s) d -> m (s d)", s=2)).then_inc(vec_in, 16)
            for i in range(NT):
                sp.dma_start(xs[:, i, :], x_d[i * P:(i + 1) * P, :]).then_inc(x_in, 16)
                if i == 0:
                    sp.dma_start(posi[:, :], pos_d.rearrange("a (i p) -> p (a i)", p=P),
                                 allow_slow_non_contiguous=True).then_inc(pos_in, 16)
                    sp.dma_start(brow[:, :], a["b_router"].broadcast_to([P, 32])).then_inc(brow_in, 16)
            def slot_used(n):
                kind, m = RING[n]
                done, count = {"ada": (ada_ps, m + 1), "in": (pj_ps, NT * (m + 1)), "c1": (hid_u, 1),
                               "wo": (wo_ps, NT * (m + 1))}[kind]
                sp.wait_ge(done, count)

            for n, (kind, m) in enumerate(RING):
                if n >= 2:
                    slot_used(n - 2)
                if kind == "ada":
                    src = w_ada[:, :, m * 512:(m + 1) * 512]
                elif kind == "in":
                    src = w_in[:, :, IN_COLS[m][0]:IN_COLS[m][1]]
                elif kind == "c1":
                    src = w_c1[m]
                else:
                    src = w_o[:, :, m * 512:(m + 1) * 512]
                sp.dma_start(ring_view(n), src).then_inc(ring_in[n % 2], 16)
                if n == 6:
                    for dup in range(2):
                        sp.dma_start(w2k[:, :, dup, :], a["w_cmp_k2"][0].rearrange("(j p) d -> p j d", p=P))\
                          .then_inc(w2_in, 16)
                    sp.dma_start(w2v[:, :, :], a["w_cmp_v2"][0].rearrange("(j p) d -> p j d", p=P)).then_inc(w2_in, 16)
                    sp.dma_start(wr[:, :, :], a["w_router"][0].rearrange("(k p) e -> p k e", p=P)).then_inc(wr_in, 16)

            def load_up(y, par, e, dst):
                src = w_up[y][:, bass.ds(e, 1)] if not isinstance(e, int) else w_up[y][:, e:e + 1]
                for h in range(2):
                    sp.dma_start(dst[:, :, h, :], src[:, :, :, h, :].rearrange("p e k c -> p (e k) c"))\
                      .then_inc((a_in, b_in)[y][par], 16)

            def load_dn(y, e):
                src = w_dn[y][:, bass.ds(e, 1)] if not isinstance(e, int) else w_dn[y][:, e:e + 1]
                for h in range(2):
                    sp.dma_start(dnw[:, y, h], src[:, :, h].rearrange("p e q n -> p (e q) n")).then_inc(d_in[y], 16)

            def load_bias(par, e):
                src = bias_d[bass.ds(e, 1)] if not isinstance(e, int) else bias_d[e:e + 1]
                sp.dma_start(biasw[:, par, :], src.rearrange("e s n -> (e s) n")).then_inc(biasw_in[par], 16)

            sp.wait_ge(oc_sb, 4)
            load_up(0, 0, 0, upw[0][0])
            slot_used(len(RING) - 2)
            slot_used(len(RING) - 1)
            load_up(1, 0, 0, upw[0][1])
            for i in range(NT):
                sp.wait_ge(x2_ready, i + 1)
                sp.dma_start(x2_d[i * P:(i + 1) * P, :], xs[:, i, :]).then_inc(x2_out, 16)
            for i in range(NT):
                sp.wait_ge(xn_ready, NT + i + 1)
                sp.dma_start(xn2_d[2 * i * P:2 * (i + 1) * P, :].rearrange("(p h) n -> p (h n)", h=2), xn2[:, i, :])\
                  .then_inc(xn2_out, 16)
            sp.wait_ge(x2_out, 16 * NT)
            sp.wait_ge(xn2_out, 16 * NT)
            sp.wait_ge(logit_ps, 1)
            for y in range(2):
                load_dn(y, 0)
            sp.wait_ge(routed, 1)
            sp.wait_ge(bias_out, 16)
            load_bias(0, 0)
            load_up(0, 1, 1, upw[1][0])
            load_up(1, 1, 1, upw[1][1])
            load_bias(1, 1)

            def first_chunk(e):
                return sp.value_load(ctab[0:1, bass.ds(e + 32, 1)] if not isinstance(e, int)
                                     else ctab[0:1, e + 32:e + 33], min_val=1, max_val=64)

            def down_of(e):
                ends = first_chunk(e)
                sp.wait_ge(dn_a, ends)
                load_dn(0, e)
                sp.wait_ge(dn_b, ends)
                load_dn(1, e)

            down_of(1)
            with sp.Fori(1, N_EXP // 2) as e2:
                for par in range(2):
                    e = e2 * 2 + par
                    used = first_chunk(e - 1)
                    sp.wait_ge(up_a, used)
                    load_up(0, par, e, upw[par][0])
                    sp.wait_ge(up_b, used)
                    load_up(1, par, e, upw[par][1])
                    sp.wait_ge(dn_b, used)
                    load_bias(par, e)
                    down_of(e)
            total = first_chunk(N_EXP)
            sp.wait_ge(up_b, total)
            sp.dma_start(x2fin, x2_d.rearrange("(i p) n -> p i n", p=P)).then_inc(fin_in, 16)
            sp.wait_ge(scattered, total * 16 + 16)
            sp.dma_start(yfin, moe_d[0:2 * SEQ, :].rearrange("(i p h) n -> p i (h n)", p=P, h=2)).then_inc(fin_in, 16)
            for i in range(NT):
                sp.wait_ge(fin_ready, i + 1)
                sp.dma_start(out[i * P:(i + 1) * P, :], yfin[:, i, :]).then_inc(out_done, 16)
            sp.wait_ge(out_done, 16 * NT)

        @block.gpsimd
        def _(pool):
            pool.dma_start(bias_f[:, 0:2 * D], a["b_up"][0]).then_inc(bias_in, 16)
            pool.dma_start(bias_f[:, 2 * D:3 * D], a["b_down"][0]).then_inc(bias_in, 16)
            pool.memset(onesb, 1.0).then_inc(bconst, 1)
            pool.memset(ones_f, 1.0).then_inc(bconst, 1)
            pool.wait_ge(consts_in, 16)
            for dst, at, n in ((identb, C_ID, P), (trib, C_TRI, P), (usb, C_US, P), (mb_b, C_MB, 512), (cm_b, C_CM, P)):
                pool.tensor_copy(dst, cf[:, at:at + n]).then_inc(bconst, 1)
            pool.wait_ge(bias_in, 32)
            for part in range(3):
                pool.tensor_copy(bias_b[:, part, :], bias_f[:, :]).then_inc(bias_split, 1)
                pool.wait_ge(bias_split, 2 * part + 1)
                if part < 2:
                    pool.tensor_tensor(bias_f[:, :], bias_f[:, :], bias_b[:, part, :], ALU.subtract)\
                        .then_inc(bias_split, 1)
                    pool.wait_ge(bias_split, 2 * part + 2)
            pool.dma_start(bias_d, bias_b).then_inc(bias_out, 16)
            pool.wait_ge(bias_out, 16)
            pool.memset(blk[:, :, :, 31:32], 0.0).then_inc(blk_zero, 1)
            for hd in range(16):
                ty, h = heads[hd]
                pool.wait_ge(o_ev, hd + 1)
                dst = o_all[:, :, h * HD:(h + 1) * HD]
                pool.tensor_tensor(dst, dst, otmp[:, hd % 2], ALU.add).then_inc(o_add, 1)
                pool.wait_ge(o_add, hd + 1)
            pool.wait_ge(o_scaled, 8)
            pool.memset(zero, 0.0).then_inc(zeroed, 1)
            pool.wait_ge(zeroed, 1)
            pool.dma_start(moe_d.rearrange("(r p) n -> p r n", p=P), bc(zero, 1, (2 * SEQ + 2 * P) // P))\
                .then_inc(scattered, 16)
            pool.wait_ge(scattered, 16)
            pool.wait_ge(xn2_out, 16 * NT)

            def gather():
                pool.indirect_dma_start(xg_in, None, xn2_d, bass.IndirectOffsetOnAxis(idxg, 0)).then_inc(gathered, 16)

            pool.wait_ge(idx_ready, 1)
            gather()
            pool.wait_ge(gathered, 16)
            pool.tensor_copy(xg, xg_in).then_inc(moved, 1)
            pool.wait_ge(moved, 1)
            pool.wait_ge(idx_ready, 2)
            gather()
            pool.wait_ge(ctab_ready, 1)
            total = pool.value_load(ctab[0:1, 64:65], min_val=1, max_val=64)
            with pool.Fori(0, total) as c:
                pool.wait_ge(gathered, c * 16 + 32)
                pool.wait_ge(xg_tr, c + 1)
                pool.sem_inc(turn, 1)
                pool.tensor_copy(xg, xg_in).then_inc(moved, 1)
                pool.wait_ge(idx_ready, c + 3)
                pool.wait_ge(moved, c + 2)
                pool.sem_inc(turn, 1)
                gather()
                pool.wait_ge(y_ready, c + 1)
                pool.wait_ge(scattered, c * 16 + 16)
                pool.sem_inc(turn, 1)
                pool.indirect_dma_start(moe_d, bass.IndirectOffsetOnAxis(idxs_c, 0), ybuf, None,
                                        compute_op=ALU.add).then_inc(scattered, 16)

        @block.scalar
        def _(act_e):
            links = [0]

            def link(ins):
                links[0] += 1
                ins.then_inc(achain, 1)
                act_e.wait_ge(achain, links[0])

            def root(norm):
                act_e.wait_ge(ms_ready, norm + 1)
                act_e.activation(st[:, 2, :], st[:, 1, :], ACT.Sqrt).then_inc(root_ready, 1)

            junk = pbuf[:, 1, :]

            def square(src, col, before):
                act_e.activation(junk, src, ACT.Square, accum_out=st[:, 0, col:col + 1]).then_inc(sumsq, 1)
                act_e.wait_ge(sumsq, before + 1)

            act_e.wait_ge(c_in, 16)
            act_e.activation(ctmp[:, 0, :], cvec, ACT.Exp, scale=-1.0).then_inc(silu_e, 1)
            act_e.wait_ge(trig_in, 1)
            act_e.activation(trig, rk, ACT.Sin).then_inc(trig_ready, 1)
            act_e.wait_ge(x_in, 16 * NT)
            for i in range(NT):
                act_e.activation(xn[:, i, :], xs[:, i, :], ACT.Square, accum_out=st[:, 0, i:i + 1])\
                    .then_inc(sumsq, 1)
            root(NORM_X)

            def tile_evac(base, dst, ab):
                for kt in range(1, KT, 2):
                    act_e.wait_ge(tile_tr, base + kt + 1)
                    act_e.activation(dst[:, kt, :], ps[:, kt % 4, :], ACT.Identity, bias=ab[1][:, kt:kt + 1] if ab[1]
                                     is not None else 0.0, scale=ab[0][:, kt:kt + 1]).then_inc(ev_act, 1)

            act_e.wait_ge(ab_ready, 1)
            tile_evac(TILE_H, hT, (ab1[:, 0:8], ab1[:, 8:16]))

            def proj_evac(n):
                for i in range(NT):
                    t = PJ[n] + i
                    b = ps[:, t % 4, :]
                    act_e.wait_ge(pj_ps, t + 1)
                    if n == 0 or n == 3 or n == 4:
                        if i == 0 and n == 3:
                            act_e.wait_ge(tg_ps, at_group[("qrot", 3)] + 1)
                        if i == 0 and n == 4:
                            act_e.wait_ge(tg_ps, at_group[("kwin", 1)] + 1)
                        act_e.activation(stage[1 if n == 4 else 0][:, i, :], b, ACT.Copy).then_inc(pj_ev, 1)
                    elif n == 1:
                        if i == 0:
                            act_e.wait_ge(bias_split, 5)
                        for dup in range(2):
                            act_e.activation(kdup[:, i, :, dup, :], b[:, 0:384].rearrange("p (g d) -> p g d", d=HD),
                                             ACT.Copy)
                        act_e.activation(v_slc[:, i, :], b[:, 384:512], ACT.Copy).then_inc(pj_ev, 1)
                    elif n == 2:
                        for dup in range(2):
                            act_e.activation(
                                stage[1][:, i, 0:256].rearrange("p (g u d) -> p g u d", g=2, u=2)[:, :, dup, :],
                                b[:, 0:128].rearrange("p (g d) -> p g d", d=HD), ACT.Copy)
                        act_e.activation(v_win[:, i, :], b[:, 128:256], ACT.Copy)
                        act_e.activation(sg[:, i, :], b[:, 256:280], ACT.Exp, scale=-1.0).then_inc(pj_ev, 1)
                    else:
                        act_e.activation(v_dil[:, i, :], b, ACT.Copy).then_inc(pj_ev, 1)

            for n in range(6):
                proj_evac(n)
            act_e.wait_ge(hid_u, 1)
            act_e.activation(gel_u, ps[:, 0, 0:256], ACT.Copy).then_inc(gel_in, 1)
            act_e.wait_ge(gel_in, 2)
            act_e.activation(gel_e, gel_t, ACT.Exp, scale=-2.0 * float(np.sqrt(2.0 / np.pi))).then_inc(gel_out, 1)
            act_e.wait_ge(sc_in, 1)
            act_e.activation(p_cmp, p_cmp, ACT.Exp).then_inc(sc_exp, 1)

            def exps(u):
                i = u % 4
                w = P * (i + 1)
                act_e.wait_ge(neg_ready, u + 1)
                if u >= 4:
                    act_e.wait_ge(tr_done, u - 3)
                if u < DIL_U:
                    act_e.activation(pbuf[:, u % 4, 0:w], ps[:, u % 4, 0:w], ACT.Exp, bias=negm[:, u:u + 1],
                                     accum_out=lsum[:, u // 4, i:i + 1]).then_inc(exp_done, 1)
                else:
                    act_e.activation(pbuf[:, u % 4, 0:w], ps[:, u % 4, 0:w], ACT.Exp, bias=negm[:, u:u + 1])\
                        .then_inc(exp_done, 1)

            exps(0)
            exps(1)
            for u in range(UNITS):
                if u + 2 < UNITS:
                    exps(u + 2)
                if u >= DIL_U:
                    w = P * (u % 4 + 1)
                    act_e.wait_ge(tr_done, u + 1)
                    act_e.wait_ge(pv_done, u - 2)
                    act_e.activation(ptb[:, u % 3, 0:w], ps[:, 4 + u % 2, 0:w], ACT.Copy).then_inc(pt_act, 1)

            act_e.wait_ge(o_ev, len(heads))
            act_e.wait_ge(o_add, 16)
            act_e.wait_ge(tr_done, UNITS)
            for half in range(2):
                for i in range(NT):
                    square(o_all[:, i, half * 512:(half + 1) * 512], half * 4 + i, SQ_BEFORE[NORM_O] + half * 4 + i)
            root(NORM_O)
            tile_evac(TILE_Y, hT, (vt[:, 80:88], None))
            for i in range(NT):
                act_e.wait_ge(wo_ps, NT + i + 1)
                for m in range(2):
                    square(ps[:, 2 * i + m, :], 4 * m + i, SQ_BEFORE[NORM_Y] + 2 * i + m)
            root(NORM_Y)
            for i in range(NT):
                act_e.wait_ge(x2_ready, i + 1)
                act_e.activation(xn2[:, i, :], xs[:, i, :], ACT.Square, accum_out=st[:, 0, i:i + 1]).then_inc(sumsq, 1)
            root(NORM_H)
            act_e.wait_ge(ab_ready, 2)
            tile_evac(TILE_2, hT, (ab2[:, 0:8], ab2[:, 8:16]))
            act_e.wait_ge(gx_in, 1)
            act_e.activation(gk, gk, ACT.Exp).then_inc(gx_out, 1)

            def spread(turns):
                act_e.wait_ge(xg_tr, turns)
                for kt in range(KT):
                    src = ps[:, 2, (kt % 4) * P + (kt // 4) * SLOTS:(kt % 4) * P + (kt // 4) * SLOTS + SLOTS]
                    ins = act_e.activation(xgT[:, kt, :], src, ACT.Identity, bias=ab2[:, 8 + kt:9 + kt],
                                           scale=ab2[:, kt:kt + 1])
                ins.then_inc(xgT_ready, 1)

            spread(1)
            act_e.wait_ge(ctab_ready, 1)
            total = act_e.value_load(ctab[0:1, 64:65], min_val=1, max_val=64)
            with act_e.Fori(0, total) as c:
                act_e.wait_ge(glu_ready, c * 2 + 1)
                act_e.activation(sw_s[:, 0], sw_g[:, 0], ACT.Sigmoid, scale=ALPHA).then_inc(sig_ready, 1)
                spread(c + 2)
                act_e.wait_ge(glu_ready, c * 2 + 2)
                act_e.activation(sw_s[:, 1], sw_g[:, 1], ACT.Sigmoid, scale=ALPHA).then_inc(sig_ready, 1)
            act_e.wait_ge(fin_in, 32)
            for i in range(NT):
                act_e.activation(take(16384, D), yfin[:, i, :], ACT.Square, accum_out=fin[:, i:i + 1])\
                    .then_inc(sumsq, 1)
                act_e.wait_ge(sumsq, SQ_BEFORE[NORM_F] + i + 1)
            act_e.wait_ge(ms_ready, NORM_F + 1)
            act_e.activation(fin[:, 8:12], fin[:, 4:8], ACT.Sqrt).then_inc(root_ready, 1)

        @block.vector
        def _(v):
            links = [0]

            def link(ins):
                links[0] += 1
                ins.then_inc(chain, 1)
                v.wait_ge(chain, links[0])

            def rstd(norm, n, width):
                ss, ms, rt_, r, t = [st[:, row, 0:n] for row in range(5)]
                v.wait_ge(sumsq, SQ_BEFORE[norm + 1])
                if norm == NORM_Y:
                    link(v.tensor_tensor(ss, ss, st[:, 0, n:2 * n], ALU.add))
                v.tensor_scalar(ms, ss, 1.0 / width, EPS, ALU.mult, ALU.add).then_inc(ms_ready, 1)
                v.wait_ge(root_ready, norm + 1)
                link(v.reciprocal(r, rt_))
                link(v.tensor_tensor(t, r, r, ALU.mult))
                link(v.tensor_tensor(t, t, ms, ALU.mult))
                link(v.tensor_scalar(t, t, -0.5, 1.5, ALU.mult, ALU.add))
                link(v.tensor_tensor(r, r, t, ALU.mult))

            link(v.memset(st[:, :, :], 1.0))
            v.wait_ge(silu_e, 1)
            link(v.tensor_scalar(ctmp[:, 1, :], ctmp[:, 0, :], 1.0, None, ALU.add))
            link(v.reciprocal(ctmp[:, 2, :], ctmp[:, 1, :]))
            link(v.tensor_tensor(cvec, cvec, ctmp[:, 2, :], ALU.mult))
            v.tensor_copy(silu_c, bc(cvec, 2, 32)).then_inc(silu_ready, 1)
            v.wait_ge(pos_in, 16)
            v.wait_ge(consts_in, 16)
            link(v.tensor_copy(posf, posi))
            link(v.tensor_tensor(ang, bc(posf, 2, 8), bc(cf[:, C_INVF:C_INVF + 8], 1, NT), ALU.mult))
            C1, C2 = 6.28125, 0.00193500518798828125
            C3 = 2.0 * np.pi - C1 - C2
            for w, quarter in ((0, 0.0), (1, 0.25)):
                k = rk[:, w]
                link(v.tensor_scalar(k, ang, 1.0 / (2.0 * np.pi), quarter, ALU.mult, ALU.add))
                link(v.tensor_scalar(k, k, MAGIC, MAGIC, ALU.add, ALU.subtract))
                r = trig[:, w]
                link(v.scalar_tensor_tensor(out=r, in0=k, scalar=-C1, in1=ang, op0=ALU.mult, op1=ALU.add))
                link(v.scalar_tensor_tensor(out=r, in0=k, scalar=-C2, in1=r, op0=ALU.mult, op1=ALU.add))
                link(v.scalar_tensor_tensor(out=r, in0=k, scalar=-C3, in1=r, op0=ALU.mult, op1=ALU.add))
                link(v.tensor_scalar(r, r, quarter * 2.0 * np.pi, 3.1415925, ALU.add, ALU.min))
                ins = v.tensor_scalar(k, r, -3.1415925, None, ALU.max)
                if w == 0:
                    link(ins)
                else:
                    ins.then_inc(trig_in, 1)
            v.wait_ge(vt_ps, 1)
            link(v.tensor_copy(vt, ps[:, 7, 0:88]))
            v.tensor_copy(posT, ps[:, 7, 128:144]).then_inc(vt_sb, 1)
            rstd(NORM_X, 4, D)
            for i in range(NT):
                v.tensor_scalar(xn[:, i, :], xs[:, i, :], st[:, 3, i:i + 1], None, ALU.mult).then_inc(xn_ready, 1)

            def ada_rows(n):
                v.wait_ge(ada_ps, n + 1)
                if n >= 2:
                    v.wait_ge(modc_ps, n - 1)
                v.tensor_copy(mrow[:, n % 2, :], ps[:, 4 + n % 2, :]).then_inc(row_sb, 1)

            def ada_cols(lo, hi):
                v.wait_ge(modc_ps, hi)
                v.tensor_tensor(modc[:, 4 * lo:4 * hi], ps[:, 6, 4 * lo:4 * hi], vt[:, 4 * lo:4 * hi], ALU.add)\
                    .then_inc(modc_sb, 1)

            for n in range(4):
                ada_rows(n)
            ada_cols(0, 4)
            v.wait_ge(modc_sb, 1)
            link(v.scalar_tensor_tensor(out=ab1[:, 0:8], in0=modc[:, 8:16], scalar=1.0, in1=vt[:, 48:56],
                                        op0=ALU.add, op1=ALU.mult))
            v.tensor_copy(ab1[:, 8:16], modc[:, 0:8]).then_inc(ab_ready, 1)
            v.wait_ge(ab_ready, 1)

            def tile_evac(base, dst, ab):
                for kt in range(0, KT, 2):
                    v.wait_ge(tile_tr, base + kt + 1)
                    v.tensor_scalar(dst[:, kt, :], ps[:, kt % 4, :], ab[0][:, kt:kt + 1],
                                    ab[1][:, kt:kt + 1] if ab[1] is not None else None, ALU.mult,
                                    ALU.add if ab[1] is not None else ALU.bypass).then_inc(ev_dve, 1)

            tile_evac(TILE_H, hT, (ab1[:, 0:8], ab1[:, 8:16]))
            v.wait_ge(trig_ready, 1)

            def rope(view, n, heads_n):
                x1, x2 = view[:, :, :, 0:8], view[:, :, :, 8:16]
                cos, sin = bc(trig[:, 1], 2, heads_n), bc(trig[:, 0], 2, heads_n)
                tb = [rope_t[:, m, 0:NT * heads_n * 8].rearrange("p (i h d) -> p i h d", i=NT, h=heads_n)
                      for m in range(4)]
                for dst, src, w in ((0, x1, cos), (1, x2, sin), (2, x2, cos), (3, x1, sin)):
                    ins = v.tensor_tensor(tb[dst], src, w, ALU.mult)
                link(ins)
                v.tensor_tensor(x1, tb[0], tb[1], ALU.subtract)
                v.tensor_tensor(x2, tb[2], tb[3], ALU.add).then_inc(roped, 1)
                v.wait_ge(roped, n)

            def group_evac(g):
                kind, j = GROUPS[g]
                v.wait_ge(tg_ps, g + 1)
                b = ps[:, 4 + g % 4, :]
                if kind in ("qraw", "qrot", "qdil"):
                    dst = {"qraw": qraw, "qrot": qrot, "qdil": qdil}[kind][:, j, :]
                    v.tensor_scalar(dst, b, HD ** -0.5, None, ALU.mult).then_inc(tg_ev, 1)
                elif kind == "dup" and j < 4:
                    if j == 0:
                        v.wait_ge(bias_out, 16)
                    v.tensor_copy(kc[0:HD, j, :], b[0:HD, :])
                    v.tensor_copy(kc[HD:P, j, 0:SEQ - 1], b[HD:P, 1:SEQ]).then_inc(tg_ev, 1)
                else:
                    dst = kslc[:, j - 4, :] if kind == "dup" else kwin[:, j, :] if kind == "kwin" else kdil[:, j, :]
                    v.tensor_copy(dst, b).then_inc(tg_ev, 1)

            def heads_of(buf):
                return buf.rearrange("p i (h d) -> p i h d", d=HD)

            for g in range(0, 4):
                group_evac(g)
            rope(heads_of(stage[0]), 1, 8)
            v.wait_ge(pj_ev, PJ[1] + NT)
            rope(kdup[:, :, 4:6].rearrange("p i g u d -> p i (g u) d"), 2, 4)
            for g in range(4, 14):
                group_evac(g)
            v.wait_ge(pj_ev, PJ[2] + NT)
            rope(heads_of(stage[1][:, :, 0:256]), 3, 4)
            for g in range(14, 16):
                group_evac(g)
            v.wait_ge(pj_ev, PJ[3] + NT)
            rope(heads_of(stage[0]), 4, 8)
            for g in range(16, 20):
                group_evac(g)
            v.wait_ge(pj_ev, PJ[4] + NT)
            rope(heads_of(stage[1]), 5, 8)
            for g in range(20, 24):
                group_evac(g)
            link(v.tensor_scalar(sg, sg, 1.0, None, ALU.add))
            link(v.reciprocal(sg, sg))
            v.wait_ge(tg_ev, len(GROUPS))
            v.wait_ge(blk_zero, 1)
            v.wait_ge(vt_sb, 1)
            for q in range(4):
                src = bass.AP(kc.tensor, kc.offset + q * SEQ, [[kc.ap[0][0], P], [2, 16], [16, 31]])
                ins = v.tensor_tensor(blk[:, :, q, 0:31], src, bc(posT, 2, 31), ALU.add)
            ins.then_inc(blk_ready, 1)
            v.wait_ge(gel_in, 1)
            link(v.tensor_tensor(gel_t, gel_u, gel_u, ALU.mult))
            link(v.tensor_scalar(gel_t, gel_t, 0.044715, 1.0, ALU.mult, ALU.add))
            v.tensor_tensor(gel_t, gel_t, gel_u, ALU.mult).then_inc(gel_in, 1)
            v.wait_ge(gel_out, 1)
            link(v.tensor_scalar(gel_e, gel_e, 1.0, None, ALU.add))
            link(v.reciprocal(gel_e, gel_e))
            v.tensor_tensor(gel_u, gel_u, gel_e, ALU.mult).then_inc(hid_ready, 1)
            v.wait_ge(hid_tr, 1)
            hps = ps[:, 1, 0:256].rearrange("p (j q) -> p j q", j=2)
            v.tensor_copy(hidT, hps)
            for g in range(2):
                src = bc(hps[:, :, 64 + 32 * g:96 + 32 * g], 2, 4)
                ins = v.tensor_copy(hidv[:, :, g], src)
            ins.then_inc(hid_sb, 1)
            v.wait_ge(cv_ps, 1)
            v.tensor_copy(kcT, ps[:, 2, 0:64].rearrange("p (g c) -> p g c", g=2))
            v.tensor_copy(vc4, ps[:, 2, 64:192].rearrange("p (g d) -> p g d", g=2)).then_inc(cv_sb, 1)
            v.wait_ge(sc_ps, 1)
            s_view = ps[:, 4:6, :].rearrange("p b (i h c) -> p (b i h) c", h=8, c=32)
            p_view = p_cmp.rearrange("p i (h c) -> p (i h) c", c=32)
            m32, l32, g32 = [sc8[:, m].rearrange("p i h -> p (i h)") for m in range(3)]
            link(v.tensor_reduce(m32, s_view, AX.X, ALU.max, negate=True))
            v.tensor_tensor(p_view, s_view, bc(m32, 2, 32), ALU.add).then_inc(sc_in, 1)
            v.wait_ge(sc_exp, 1)
            link(v.tensor_reduce(l32, p_view, AX.X, ALU.add))
            link(v.reciprocal(l32, l32))
            sg4 = sg.rearrange("p i (h t) -> p i h t", t=3)
            link(v.tensor_tensor(sc8[:, 2], sc8[:, 1], sg4[:, :, :, 0], ALU.mult))
            link(v.tensor_tensor(p_view, p_view, bc(g32, 2, 32), ALU.mult))
            valid = cf[:, C_CV:C_CV + P].rearrange("p (i c) -> p i c", c=32)
            v.tensor_tensor(p_cmp.rearrange("p i (h c) -> p i h c", c=32), p_cmp.rearrange("p i (h c) -> p i h c", c=32),
                            bc(valid, 2, 8), ALU.mult).then_inc(pc_ready, 1)
            v.wait_ge(pc_tr, 1)
            v.tensor_copy(pcT, ps[:, 6:8, :].rearrange("p g (i q) -> p g i q", i=NT)).then_inc(pc_sb, 1)
            for i in range(NT):
                v.wait_ge(oc_ps, 1)
                v.tensor_copy(o_all[:, i, 0:512], ps[:, i, :]).then_inc(oc_sb, 1)
            for n in range(4, 12):
                ada_rows(n)
            ada_cols(4, 12)
            v.wait_ge(modc_sb, 2)
            link(v.scalar_tensor_tensor(out=ab2[:, 0:8], in0=modc[:, 32:40], scalar=1.0, in1=vt[:, 64:72],
                                        op0=ALU.add, op1=ALU.mult))
            v.tensor_copy(ab2[:, 8:16], modc[:, 24:32]).then_inc(ab_ready, 1)
            link(v.tensor_tensor(modc[:, 16:24], modc[:, 16:24], vt[:, 56:64], ALU.mult))
            link(v.tensor_tensor(modc[:, 40:48], modc[:, 40:48], vt[:, 72:80], ALU.mult))

            def row_max(u):
                w = P * (u % 4 + 1)
                v.wait_ge(qk_done, u + 1)
                v.tensor_reduce(negm[:, u:u + 1], ps[:, u % 4, 0:w], AX.X, ALU.max, negate=True).then_inc(neg_ready, 1)

            def weigh(u):
                i = u % 4
                w = P * (i + 1)
                v.wait_ge(exp_done, u + 1)
                pb = pbuf[:, u % 4, 0:w]
                v.tensor_tensor_reduce(pb, pb, cf[:, C_MULT + (3 - i) * P:C_MULT + 512], 1.0, 0.0, ALU.mult, ALU.add,
                                       lsum[:, u // 4, i:i + 1]).then_inc(mul_done, 1)

            def pt_evac(u):
                w = P * (u % 4 + 1)
                v.wait_ge(tr_done, u + 1)
                if u >= 3:
                    v.wait_ge(pv_done, u - 2)
                v.tensor_copy(ptb[:, u % 3, 0:w], ps[:, 4 + u % 2, 0:w]).then_inc(pt_dve, 1)

            def o_evac(hd):
                ty, h = heads[hd]
                v.wait_ge(pv_done, 4 * hd + 4)
                if hd < 16:
                    v.wait_ge(exp_done, 4 * hd + 4)
                else:
                    v.wait_ge(mul_done, 4 * (hd - 16) + 4)
                r = osc[:, 0, hd % 2, :]
                link(v.reciprocal(r, lsum[:, hd, :]))
                src = ps[:, 6 + hd % 2, 0:256].rearrange("p (i d) -> p i d", d=HD)
                if ty == N_DIL:
                    v.tensor_tensor(o_all[:, :, 512 + h * HD:512 + (h + 1) * HD], src, bc(r, 2, HD), ALU.mult)\
                        .then_inc(o_ev, 1)
                    return
                s = osc[:, 1, hd % 2, :]
                link(v.tensor_tensor(s, r, sg4[:, :, h, ty + 1], ALU.mult))
                if hd >= 2:
                    v.wait_ge(o_add, hd - 1)
                v.tensor_tensor(otmp[:, hd % 2], src, bc(s, 2, HD), ALU.mult).then_inc(o_ev, 1)

            for u in range(3):
                row_max(u)
            for u in range(UNITS):
                if u + 3 < UNITS:
                    row_max(u + 3)
                if u >= DIL_U:
                    weigh(u)
                else:
                    pt_evac(u)
                if u % 4 == 1 and u > 4:
                    o_evac(u // 4 - 1)
            o_evac(len(heads) - 1)

            rstd(NORM_O, 8, 512)
            for half in range(2):
                for i in range(NT):
                    o = o_all[:, i, half * 512:(half + 1) * 512]
                    v.tensor_scalar(o, o, st[:, 3, half * 4 + i:half * 4 + i + 1], None, ALU.mult)\
                        .then_inc(o_scaled, 1)
            tile_evac(TILE_Y, hT, (vt[:, 80:88], None))
            for m, col in enumerate((16, 40)):
                for half in range(2):
                    n = 2 * m + half
                    if n:
                        v.wait_ge(diag_ps, n)
                    for q in range(4):
                        kt = 4 * half + q
                        ins = v.tensor_scalar(diag[:, q, :], ident, modc[:, col + kt:col + kt + 1], None, ALU.mult)
                    ins.then_inc(diag_ready, 1)
                    v.wait_ge(diag_ps, n + 1)
                    dst = (gbm, gbf)[m][:, half * 512:(half + 1) * 512]
                    v.tensor_copy(dst, ps[:, 4, :]).then_inc(gb_sb, 1)
                    v.wait_ge(gb_sb, n + 1)
            rstd(NORM_Y, 4, D)
            v.wait_ge(wo_ps, 2 * NT)
            for i in range(NT):
                y = o_all[:, i, :]
                link(v.scalar_tensor_tensor(out=y.rearrange("p (m n) -> p m n", m=2), in0=ps[:, 2 * i:2 * i + 2, :],
                                            scalar=st[:, 3, i:i + 1], in1=gbm.rearrange("p (m n) -> p m n", m=2),
                                            op0=ALU.mult, op1=ALU.mult))
                v.tensor_tensor(xs[:, i, :], xs[:, i, :], y, ALU.add).then_inc(x2_ready, 1)
            v.wait_ge(x2_ready, NT)
            rstd(NORM_H, 4, D)
            for i in range(NT):
                v.tensor_scalar(xn2[:, i, :], xs[:, i, :], st[:, 3, i:i + 1], None, ALU.mult).then_inc(xn_ready, 1)
            tile_evac(TILE_2, hT, (ab2[:, 0:8], ab2[:, 8:16]))

            v.wait_ge(logit_ps, 1)
            link(v.tensor_tensor(lg, ps[:, 4, 0:P].rearrange("p (i e) -> p i e", e=32), bc(brow, 1, NT), ALU.add))
            for i in range(NT):
                ins = v.max(top8[:, i, :], lg[:, i, :])
            link(ins)
            for i in range(NT):
                ins = v.max_index(idx8[:, i, :], top8[:, i, :], lg[:, i, :])
            link(ins)
            v.tensor_tensor(gk, top8[:, :, 0:TOP_K], top8[:, :, 0:1].broadcast_to([P, NT, TOP_K]), ALU.subtract)\
                .then_inc(gx_in, 1)
            link(v.tensor_copy(eidx, idx8[:, :, 0:TOP_K]))
            link(v.tensor_tensor(onehot, bc(cf[:, C_I32:C_I32 + 32], 1, 16),
                                 bc(eidx.rearrange("p i k -> p (i k)"), 2, 32), ALU.is_equal))
            oh4 = onehot.rearrange("p (i k) e -> p i k e", k=TOP_K)
            with nc.allow_low_precision("sums of zeros and ones are exact"):
                v.tensor_reduce(maskb, onehot.rearrange("p (i k) e -> p i e k", k=TOP_K), AX.X, ALU.add)\
                    .then_inc(mask_ready, 1)
            v.wait_ge(count_ps, 1)
            link(v.tensor_scalar(cnt, ps[:, 6, 0:32], 1.0 / SLOTS, (SLOTS - 1.0) / SLOTS - 0.5 + 0.5 / SLOTS,
                                 ALU.mult, ALU.add))
            link(v.tensor_scalar(nch, cnt, MAGIC, MAGIC, ALU.add, ALU.subtract))
            link(v.tensor_scalar(nch, nch, 1.0, None, ALU.max))
            v.memset(scan[0][:, 0:16], 0.0)
            v.memset(scan[1][:, 0:16], 0.0)
            link(v.tensor_copy(scan[0][:, 16:48], nch))
            for s in range(5):
                src, dst = scan[s % 2], scan[(s + 1) % 2]
                link(v.tensor_tensor(dst[:, 16:48], src[:, 16:48], src[:, 16 - (1 << s):48 - (1 << s)], ALU.add))
            last = scan[1]
            v.tensor_copy(ctab[0:1, 64:65], last[0:1, 47:48])
            v.tensor_copy(ctab[0:1, 0:32], nch[0:1, :])
            link(v.tensor_tensor(cnt, last[:, 16:48], nch, ALU.subtract))
            v.tensor_copy(ctab[0:1, 32:64], cnt[0:1, :]).then_inc(ctab_ready, 1)
            v.wait_ge(ctab_ready, 1)
            link(v.tensor_scalar(cnt, cnt, float(SLOTS), None, ALU.mult))
            link(v.tensor_tensor(flat_e, ps[:, 5, 0:P].rearrange("p (i e) -> p i e", e=32), bc(cnt, 1, NT), ALU.add))
            link(v.tensor_tensor(prod.rearrange("p (i k) e -> p i k e", k=TOP_K), oh4, bc(flat_e, 2, TOP_K), ALU.mult))
            link(v.tensor_reduce(flatk, prod, AX.X, ALU.add))
            v.wait_ge(gx_out, 1)
            link(v.tensor_reduce(gsum, gk, AX.X, ALU.add))
            link(v.reciprocal(gsum, gsum))
            link(v.tensor_tensor(gk, gk, bc(gsum, 2, TOP_K), ALU.mult))
            gflat = gk.rearrange("p i k -> p (i k)")
            for part in range(3):
                link(v.tensor_copy(ghi[:, part], gflat))
                v.tensor_copy(rt[:, :, 3 + part], ghi[:, part])
                if part < 2:
                    link(v.tensor_tensor(gflat, gflat, ghi[:, part], ALU.subtract))
            v.tensor_copy(rt[:, :, 0:3], cf[:, C_RT:C_RT + 48].rearrange("p (n c) -> p n c", c=3)).then_inc(routed, 1)

            iota_b = bc(cf[:, C_IOTA:C_IOTA + P], 1, 16)

            def pick():
                v.tensor_tensor(sel, iota_b, bc(flatk, 2, P), ALU.is_equal).then_inc(sel_ready, 1)

            pick()
            v.wait_ge(sel_ready, 1)
            link(v.tensor_scalar(flatk, flatk, float(SLOTS), None, ALU.subtract))

            def indices(step, m):
                step(v.tensor_copy(mraw, ps[:, 6, 0:6]))
                v.tensor_tensor(mt[:, 1:2], mraw[:, 3:4], mraw[:, 4:5], ALU.add)
                step(v.tensor_tensor(mt[:, 0:1], mraw[:, 0:1], mraw[:, 1:2], ALU.add))
                v.tensor_tensor(gate_all[:, m], mt[:, 1:2], mraw[:, 5:6], ALU.add)
                v.tensor_scalar(idxg, mt[:, 0:1], 2.0, cf[:, C_HALF:C_HALF + 1], ALU.mult, ALU.add)
                step(v.tensor_scalar(mt[:, 2:3], mt[:, 0:1], 2.0, cf[:, C_PADH:C_PADH + 1], ALU.mult, ALU.add))
                v.scalar_tensor_tensor(out=row_all[:, m], in0=mraw[:, 2:3], scalar=cf[:, C_NEGP:C_NEGP + 1],
                                       in1=mt[:, 2:3], op0=ALU.mult, op1=ALU.add).then_inc(idx_ready, 1)

            for m in range(2):
                v.wait_ge(sel_ps, m + 1)
                if m:
                    v.wait_ge(gathered, 16)
                indices(link, slice(m, m + 1))
                pick()
                v.wait_ge(sel_ready, m + 2)
                if m == 0:
                    link(v.tensor_scalar(flatk, flatk, float(SLOTS), None, ALU.subtract))
            v.wait_ge(ctab_ready, 1)
            total = v.value_load(ctab[0:1, 64:65], min_val=1, max_val=64)
            BASE = links[0]
            PER = 9
            with v.Fori(0, total) as c:
                n_in = [0]
                base = v.snap(c * PER + BASE)

                def step(ins):
                    n_in[0] += 1
                    ins.then_inc(chain, 1)
                    v.wait_ge(chain, base + n_in[0])

                def glu(y):
                    up = ps[:, y, :].rearrange("p (n two) -> p n two", two=2)
                    v.wait_ge((up_a, up_b)[y], c + 1)
                    v.tensor_scalar(sw_g[:, y], up[:, :, 0], LIMIT, None, ALU.min).then_inc(glu_ready, 1)
                    step(v.tensor_scalar(sw_l, up[:, :, 1], LIMIT, -LIMIT, ALU.min, ALU.max))
                    v.wait_ge(glu_ready, c * 2 + y + 1)
                    step(v.scalar_tensor_tensor(out=sw_t, in0=sw_l, scalar=1.0, in1=sw_g[:, y], op0=ALU.add,
                                                op1=ALU.mult))
                    v.wait_ge(sig_ready, c * 2 + y + 1)
                    v.tensor_tensor(act[:, y], sw_t, sw_s[:, y], ALU.mult).then_inc(act_ready, 1)

                def turn_out(y):
                    v.wait_ge(act_tr, c * 2 + y + 1)
                    v.tensor_copy(actT[:, y], ps[:, 3 + y, 0:256].rearrange("p (q s) -> p q s", q=2))\
                        .then_inc(actT_ready, 1)

                glu(0)
                v.wait_ge(sel_ps, c + 3)
                v.wait_ge(gathered, c * 16 + 32)
                indices(step, bass.ds(c + 2, 1))
                step(v.tensor_scalar(flatk, flatk, float(SLOTS), None, ALU.subtract))
                pick()
                turn_out(0)
                glu(1)
                turn_out(1)
                v.wait_ge(scattered, c * 16 + 16)
                v.wait_ge(idx_ready, c + 1)
                v.tensor_copy(idxs_c, row_all[:, bass.ds(c, 1)])
                step(v.tensor_copy(gate_c, gate_all[:, bass.ds(c, 1)]))
                v.wait_ge(dn_b, c + 1)
                v.tensor_scalar(ybuf, ps[:, 5, :], gate_c, None, ALU.mult).then_inc(y_ready, 1)
            assert n_in[0] == PER
            v.wait_ge(sumsq, SQ_BEFORE[NORM_F] + 4)
            v.tensor_scalar(fin[:, 4:8], fin[:, 0:4], 1.0 / D, EPS, ALU.mult, ALU.add).then_inc(ms_ready, 1)
            v.wait_ge(root_ready, NORM_F + 1)
            tail = [0]

            def tstep(ins):
                tail[0] += 1
                ins.then_inc(tail_chain, 1)
                v.wait_ge(tail_chain, tail[0])

            r, t, ms = fin[:, 8:12], fin[:, 12:16], fin[:, 4:8]
            tstep(v.reciprocal(r, fin[:, 8:12]))
            tstep(v.tensor_tensor(t, r, r, ALU.mult))
            tstep(v.tensor_tensor(t, t, ms, ALU.mult))
            tstep(v.tensor_scalar(t, t, -0.5, 1.5, ALU.mult, ALU.add))
            tstep(v.tensor_tensor(r, r, t, ALU.mult))
            for i in range(NT):
                tstep(v.scalar_tensor_tensor(out=yfin[:, i, :], in0=yfin[:, i, :], scalar=r[:, i:i + 1], in1=gbf,
                                             op0=ALU.mult, op1=ALU.mult))
                v.tensor_tensor(yfin[:, i, :], yfin[:, i, :], x2fin[:, i, :], ALU.add).then_inc(fin_ready, 1)

        @block.tensor
        def _(pe):
            pe.wait_ge(consts_in, 16)
            pe.wait_ge(vec_in, 16 * 8)
            pe.transpose(ps[:, 7, 0:88], vr, ident[0:88, 0:88])
            pe.transpose(ps[:, 7, 128:144], cposr, ident[0:16, 0:16]).then_inc(vt_ps, 1)
            pe.wait_ge(silu_ready, 1)

            def arrived(item):
                n = at_ring[item]
                pe.wait_ge(ring_in[n % 2], 16 * (n // 2 + 1))
                return ring_view(n)

            def ada(n):
                w = arrived(("ada", n))
                if n >= 2:
                    pe.wait_ge(row_sb, n - 1)
                for j in range(KT):
                    g = j % 4
                    ins = pe.matmul(ps[32 * g:32 * g + 32, 4 + n % 2, :], silu_c[:, j, :], w[:, j, :],
                                    start=(j < 4), stop=(j >= 4))
                ins.then_inc(ada_ps, 1)

            def ada_t(n):
                pe.wait_ge(row_sb, n + 1)
                for q in range(4):
                    ins = pe.matmul(ps[:, 6, 4 * n + q:4 * n + q + 1], mrow[:, n % 2, q * P:(q + 1) * P],
                                    cf[:, C_SEL4:C_SEL4 + 1], start=True, stop=True)
                ins.then_inc(modc_ps, 1)

            for n in range(4):
                ada(n)
                if n:
                    ada_t(n - 1)
            ada_t(3)

            def turn_tiles(base, src, ready, count):
                for kt in range(KT):
                    if kt >= 4:
                        pe.wait_ge((ev_dve, ev_act)[kt % 2], (base + kt - 4) // 2 + 1)
                    for i in range(NT):
                        if kt == 0:
                            pe.wait_ge(ready, count(i))
                        ins = pe.transpose(ps[:, kt % 4, i * P:(i + 1) * P], src[:, i, kt * P:(kt + 1) * P], ident)
                    ins.then_inc(tile_tr, 1)

            turn_tiles(TILE_H, xn, xn_ready, lambda i: i + 1)
            pe.wait_ge(ev_dve, 4)
            pe.wait_ge(ev_act, 4)

            def project(n):
                w = arrived(("in", n))
                width = IN_COLS[n][1] - IN_COLS[n][0]
                for i in range(NT):
                    t = PJ[n] + i
                    if t >= 4:
                        pe.wait_ge(pj_ev, t - 3)
                    for kt in range(KT):
                        ins = pe.matmul(ps[:, t % 4, 0:width], hT[:, kt, i * P:(i + 1) * P], w[:, kt, :],
                                        start=(kt == 0), stop=(kt == KT - 1))
                    ins.then_inc(pj_ps, 1)

            def turn_group(g):
                kind, j = GROUPS[g]
                if g >= 4:
                    pe.wait_ge(tg_ev, g - 3)
                for i in range(NT):
                    if kind == "dup":
                        src = kdup[:, i, j].rearrange("p u d -> p (u d)")
                    else:
                        buf = stage[{"qraw": 0, "qrot": 0, "kwin": 1, "qdil": 0, "kdil": 1}[kind]]
                        src = buf[:, i, j * P:(j + 1) * P]
                    ins = pe.transpose(ps[:, 4 + g % 4, i * P:(i + 1) * P], src, ident)
                ins.then_inc(tg_ps, 1)

            project(0)
            project(1)
            pe.wait_ge(pj_ev, PJ[0] + NT)
            for g in range(0, 4):
                turn_group(g)
            project(2)
            pe.wait_ge(roped, 1)
            for g in range(4, 8):
                turn_group(g)
            pe.wait_ge(roped, 2)
            for g in range(8, 14):
                turn_group(g)
            project(3)
            pe.wait_ge(roped, 3)
            for g in range(14, 16):
                turn_group(g)
            project(4)
            pe.wait_ge(roped, 4)
            for g in range(16, 20):
                turn_group(g)
            project(5)
            pe.wait_ge(roped, 5)
            for g in range(20, 24):
                turn_group(g)
            pe.wait_ge(blk_ready, 1)
            wk, wv = arrived(("c1", 0)), arrived(("c1", 1))
            pe.wait_ge(pj_ev, 4 * 6)
            for m in range(16):
                pe.matmul(ps[0:64, 0, 0:256], blk[:, m, 0:2, :], wk[:, m, :], start=(m == 0), stop=(m == 15))
                ins = pe.matmul(ps[64:128, 0, 0:256], blk[:, m, 2:4, :], wv[:, m, :], start=(m == 0), stop=(m == 15))
            ins.then_inc(hid_u, 1)
            pe.wait_ge(gel_in, 1)
            pe.wait_ge(hid_ready, 1)
            for j in range(2):
                ins = pe.transpose(ps[:, 1, j * P:(j + 1) * P], gel_u[:, j * P:(j + 1) * P], ident)
            ins.then_inc(hid_tr, 1)
            pe.wait_ge(hid_sb, 1)
            pe.wait_ge(w2_in, 48)
            for j in range(2):
                pe.matmul(ps[:, 2, 0:64], w2k[:, j].rearrange("p u d -> p (u d)"), hidT[:, j, 0:64],
                          start=(j == 0), stop=(j == 1))
            for g in range(2):
                for j in range(2):
                    ins = pe.matmul(ps[:, 2, 64 + g * HD:64 + (g + 1) * HD],
                                    hidv[:, j, g].rearrange("p r c -> p (r c)"), w2v[:, j, :],
                                    start=(j == 0), stop=(j == 1))
            ins.then_inc(cv_ps, 1)
            pe.wait_ge(cv_sb, 1)
            pe.wait_ge(bconst, 7)
            pe.wait_ge(tg_ev, len(GROUPS))
            for i in range(NT):
                rhs = bc(cm_b[:, 32 * i:32 * (i + 1)], 1, 8)
                pe.matmul(ps[:, 4 + i // 2, (i % 2) * 256:(i % 2 + 1) * 256], identb, rhs, start=(i % 2 == 0),
                          stop=False, skip_group_check=True)
            for odd in range(2):
                for pair in range(4):
                    h = 2 * pair + odd
                    off = HD * odd
                    for i in range(NT):
                        at = (i % 2) * 256 + h * 32
                        ins = pe.matmul(ps[:, 4 + i // 2, at:at + 32], qraw[off:off + HD, pair, i * P:(i + 1) * P],
                                        kcT[off:off + HD, h // 4, :], start=False, stop=(odd == 1 and pair == 3),
                                        skip_group_check=True)
                if odd == 0:
                    ins.then_inc(row_turn, 1)
                    pe.wait_ge(row_turn, 1)
            ins.then_inc(sc_ps, 1)
            pe.wait_ge(pc_ready, 1)
            for g in range(2):
                for i in range(NT):
                    ins = pe.transpose(ps[:, 6 + g, i * P:(i + 1) * P], p_cmp[:, i, g * P:(g + 1) * P], ident)
            ins.then_inc(pc_tr, 1)
            pe.wait_ge(pc_sb, 1)
            for r in range(4):
                for g in range(2):
                    for i in range(NT):
                        h = 4 * g + r
                        ins = pe.matmul(ps[:, i, h * HD:(h + 1) * HD], pcT[32 * r:32 * r + 32, g, i, :],
                                        vc4[32 * r:32 * r + 32, g, :], start=True, stop=True)
                if r < 3:
                    ins.then_inc(row_turn, 1)
                    pe.wait_ge(row_turn, r + 2)
            ins.then_inc(oc_ps, 1)
            for n in range(4, 12):
                ada(n)
                if n > 4:
                    ada_t(n - 1)
            ada_t(11)
            pe.wait_ge(modc_sb, 2)
            pe.wait_ge(oc_sb, 4)

            def qk(u):
                ty, h = heads[u // 4]
                i = u % 4
                w = P * (i + 1)
                if u >= 4:
                    pe.wait_ge(exp_done, u - 3)
                off = HD * (h % 2)
                q = (qdil if ty == N_DIL else qrot)[off:off + HD, h // 2, i * P:(i + 1) * P]
                k = (kslc[off:off + HD, h // 4], kwin[off:off + HD, h // 4], kdil[off:off + HD, h // 2])[ty][:, 0:w]
                pe.matmul(ps[:, u % 4, 0:w], q, k, start=True, stop=False)
                if ty == N_DIL:
                    ins = pe.matmul(ps[:, u % 4, 0:w], identb, mb_b[:, (3 - i) * P:512], start=False, stop=True)
                else:
                    ins = pe.matmul(ps[:, u % 4, i * P:w], identb, trib, start=False, stop=True)
                ins.then_inc(qk_done, 1)

            def copied(u):
                if u < DIL_U:
                    pe.wait_ge(pt_dve, u + 1)
                else:
                    pe.wait_ge(pt_act, u - DIL_U + 1)

            def turn(u):
                if u < DIL_U:
                    pe.wait_ge(exp_done, u + 1)
                else:
                    pe.wait_ge(mul_done, u - DIL_U + 1)
                if u >= 2:
                    copied(u - 2)
                for kb in range(u % 4 + 1):
                    ins = pe.transpose(ps[:, 4 + u % 2, kb * P:(kb + 1) * P], pbuf[:, u % 4, kb * P:(kb + 1) * P], ident)
                ins.then_inc(tr_done, 1)

            def pv(u):
                ty, h = heads[u // 4]
                hd, i = u // 4, u % 4
                copied(u)
                if i == 0 and hd >= 2:
                    pe.wait_ge(o_ev, hd - 1)
                val, col = ((v_slc, h // 4 * HD), (v_win, h // 4 * HD), (v_dil, h * HD))[ty]
                for kb in range(i + 1):
                    ins = pe.matmul(ps[:, 6 + hd % 2, i * HD:(i + 1) * HD], ptb[:, u % 3, kb * P:(kb + 1) * P],
                                    val[:, kb, col:col + HD], start=(kb == 0), stop=(kb == i))
                ins.then_inc(pv_done, 1)

            for u in range(3):
                qk(u)
            for u in range(UNITS):
                if u + 3 < UNITS:
                    qk(u + 3)
                turn(u)
                if u:
                    pv(u - 1)
            pv(UNITS - 1)

            turn_tiles(TILE_Y, o_all, o_scaled, lambda i: 8)
            for m in range(2):
                for half in range(2):
                    pe.wait_ge(diag_ready, 2 * m + half + 1)
                    for q in range(4):
                        ins = pe.matmul(ps[:, 4, q * P:(q + 1) * P], ones_f, diag[:, q, :], start=True, stop=True)
                    ins.then_inc(diag_ps, 1)
            pe.wait_ge(gb_sb, 4)
            pe.wait_ge(ev_dve, 8)
            pe.wait_ge(ev_act, 8)
            for n in range(2):
                w = arrived(("wo", n))
                for i in range(NT):
                    for kt in range(KT):
                        ins = pe.matmul(ps[:, 2 * i + n, :], hT[:, kt, i * P:(i + 1) * P], w[:, kt, :],
                                        start=(kt == 0), stop=(kt == KT - 1))
                    ins.then_inc(wo_ps, 1)
            pe.wait_ge(x2_ready, NT)
            turn_tiles(TILE_2, xn2, xn_ready, lambda i: NT + i + 1)
            pe.wait_ge(ev_dve, 12)
            pe.wait_ge(ev_act, 12)
            pe.wait_ge(wr_in, 16)
            for i in range(NT):
                for kt in range(KT):
                    ins = pe.matmul(ps[:, 4, 32 * i:32 * (i + 1)], hT[:, kt, i * P:(i + 1) * P], wr[:, kt, :],
                                    start=(kt == 0), stop=(kt == KT - 1))
            ins.then_inc(logit_ps, 1)
            pe.wait_ge(mask_ready, 1)
            for i in range(NT):
                for j in range(i + 1):
                    pe.matmul(ps[:, 5, 32 * i:32 * (i + 1)], usb if j == i else onesb, maskb[:, j, :],
                              start=(j == 0), stop=(j == i))
            for i in range(NT):
                ins = pe.matmul(ps[:, 6, 0:32], onesb, maskb[:, i, :], start=(i == 0), stop=(i == NT - 1))
            ins.then_inc(count_ps, 1)

            def pick_sum():
                for n in range(16):
                    ins = pe.matmul(ps[:, 6, 0:6], sel[:, n, :], rt[:, n, :], start=(n == 0), stop=(n == 15))
                ins.then_inc(sel_ps, 1)

            def turn_rows():
                for q in range(4):
                    ins = pe.transpose(ps[:, 2, q * P:(q + 1) * P], xg[:, q * P:(q + 1) * P], ident)
                ins.then_inc(xg_tr, 1)

            for m in range(2):
                pe.wait_ge(sel_ready, m + 1)
                if m:
                    pe.wait_ge(idx_ready, m)
                pick_sum()
            pe.wait_ge(moved, 1)
            turn_rows()
            pe.wait_ge(ctab_ready, 1)
            with pe.Fori(0, N_EXP // 2) as e2:
                for par in range(2):
                    chunks = pe.value_load(ctab[0:1, bass.ds(e2 * 2 + par, 1)], min_val=1, max_val=8)
                    first = pe.value_load(ctab[0:1, bass.ds(e2 * 2 + (par + 32), 1)], min_val=0, max_val=64)
                    weights_here = e2 * 16 + 16
                    with pe.Fori(0, chunks) as j:
                        c = first + j
                        pe.wait_ge(sel_ready, c + 3)
                        pe.wait_ge(idx_ready, c + 2)
                        pick_sum()
                        pe.wait_ge(xgT_ready, c + 1)
                        pe.wait_ge(biasw_in[par], weights_here)
                        for y in range(2):
                            pe.wait_ge((a_in, b_in)[y][par], weights_here * 2)
                            for h in range(2):
                                col = 1024 * h + 512 * y
                                pe.matmul(ps[64 * h:64 * h + 64, y, :], onesb[0:3, 0:SLOTS],
                                          biasw[:, par, col:col + 512], start=True, stop=False)
                            for kt in range(KT):
                                for h in range(2):
                                    ins = pe.matmul(ps[64 * h:64 * h + 64, y, :], xgT[:, kt, :],
                                                    upw[par][y][:, kt, h, :], start=False, stop=(kt == KT - 1))
                            ins.then_inc((up_a, up_b)[y], 1)
                        pe.wait_ge(moved, c + 2)
                        turn_rows()
                        for y in range(2):
                            pe.wait_ge(act_ready, c * 2 + y + 1)
                            for q in range(2):
                                ins = pe.transpose(ps[:, 3 + y, q * P:(q + 1) * P], act[:, y, q * P:(q + 1) * P], ident)
                            ins.then_inc(act_tr, 1)
                            if y == 0:
                                for h in range(2):
                                    pe.matmul(ps[64 * h:64 * h + 64, 5, :], onesb[0:3, 0:SLOTS],
                                              biasw[:, par, 2048 + 512 * h:2560 + 512 * h], start=True, stop=False)
                            pe.wait_ge(actT_ready, c * 2 + y + 1)
                            pe.wait_ge(d_in[y], (e2 * 2 + par) * 32 + 32)
                            for q in range(2):
                                for s in range(2):
                                    for h in range(2):
                                        last = y == 1 and q == 1 and s == 1
                                        ins = pe.matmul(ps[64 * h:64 * h + 64, 5, :],
                                                        actT[:, y, q, s * SLOTS:(s + 1) * SLOTS],
                                                        dnw[:, y, s, q, 512 * h:512 * (h + 1)],
                                                        start=False, stop=last)
                            ins.then_inc((dn_a, dn_b)[y], 1)


_INS = ["x", "c", "positions", "w_ada", "b_ada", "g_pre_mix", "g_post_mix", "g_pre_ffn", "g_post_ffn", "w_in",
        "cmp_pos", "w_cmp_k1", "w_cmp_k2", "w_cmp_v1", "w_cmp_v2", "g_out_nsa", "g_out_dil", "w_o", "w_router",
        "b_router", "w_up", "b_up", "w_down", "b_down"]


def kernel(**inputs):
    import concourse.bacc as _bacc
    from concourse.bass_utils import run_bass_kernel_spmd as _run

    nc = _bacc.Bacc("TRN2", target_bir_lowering=False, num_devices=1)
    arrays, args = {}, {}
    for name in _INS:
        arr = np.ascontiguousarray(inputs[name])
        arrays[f"in_{name}"] = arr
        args[name] = nc.dram_tensor(f"in_{name}", arr.shape, mybir.dt.from_np(arr.dtype), kind="ExternalInput").ap()
    out = nc.dram_tensor("out_y", (SEQ, D), F32, kind="ExternalOutput").ap()
    hybrid_layer(nc, args, out)
    r = _run(nc, [arrays], core_ids=[0])
    return np.asarray(r.results[0]["out_y"]).reshape(1, SEQ, D)
```

```python
from contextlib import ExitStack

import numpy as np

import concourse.bass as bass
from concourse import mybir

ALU = mybir.AluOpType
ACT = mybir.ActivationFunctionType
AX = mybir.AxisListType
F32 = mybir.dt.float32
BF16 = mybir.dt.bfloat16
I32 = mybir.dt.int32
U32 = mybir.dt.uint32

P = 128
SEQ = 512
D = 1024
NT = SEQ // P
KT = D // P
HD = 64
N_EXP = 32
TOP_K = 4
DFF = 1024
EPS = 1e-6
NEG = -1e30
SLOTS = 64
LIMIT = 7.0
ALPHA = 1.702
N_SLC, N_WIN, N_DIL = 0, 1, 2
MAGIC = 12582912.0
PAD_ROW = 1024

C_ID, C_IOTA, C_TRI, C_MB, C_MULT, C_CM, C_CV, C_US = 0, 128, 256, 384, 896, 1408, 1536, 1664
C_INVF, C_SEL4, C_RT, C_HALF, C_PADH, C_NEGP, C_I32 = 1792, 1800, 1801, 1849, 1850, 1851, 1852
C_ALL = 1884


def shape_constants():
    t = np.zeros((P, C_ALL), np.float32)
    p = np.arange(P)
    q = np.arange(P)
    t[:, C_ID:C_ID + P] = np.eye(P)
    t[:, C_IOTA:C_IOTA + P] = (q % SLOTS)[None]
    t[:, C_TRI:C_TRI + P] = np.where(q[None] <= p[:, None], 0.0, NEG)
    for blk in range(NT):
        dist = (NT - 1 - blk) * P + p[:, None] - q[None]
        mult = (dist >= 0) * ((dist <= 128).astype(int) + (dist % 4 == 0) + (dist % 16 == 0))
        t[:, C_MULT + blk * P:C_MULT + (blk + 1) * P] = mult
        t[:, C_MB + blk * P:C_MB + (blk + 1) * P] = np.where(mult > 0, 0.0, NEG)
    for i in range(NT):
        c = np.arange(32)
        ok = (c[None] * 16 + 31 <= (i * P + p)[:, None]) & (c[None] < 31)
        t[:, C_CV + 32 * i:C_CV + 32 * (i + 1)] = ok
        t[:, C_CM + 32 * i:C_CM + 32 * (i + 1)] = np.where(ok, 0.0, NEG)
    t[:, C_US:C_US + P] = p[:, None] < q[None]
    t[:, C_INVF:C_INVF + 8] = (np.float32(500000.0) ** (-np.arange(8, dtype=np.float32) / np.float32(8)))[None]
    t[::32, C_SEL4] = 1.0
    for i in range(NT):
        for k in range(TOP_K):
            c = C_RT + 3 * (i * TOP_K + k)
            t[:, c], t[:, c + 1], t[:, c + 2] = p, P * i, 1.0
    half = p // SLOTS
    t[:, C_HALF] = half
    t[:, C_PADH] = half + PAD_ROW + p
    t[:, C_NEGP] = -(PAD_ROW + p)
    t[:, C_I32:C_I32 + 32] = np.arange(32)[None]
    return t


def hybrid_layer(nc, a, out):
    x_d, c_d, pos_d = a["x"][0], a["c"], a["positions"]
    w_ada = a["w_ada"][0].rearrange("(p j) n -> p j n", j=KT)
    w_in = a["w_in"][0].rearrange("(kt p) n -> p kt n", p=P)
    w_o = a["w_o"][0].rearrange("(kt p) n -> p kt n", p=P)
    w_c1 = [a[n][0].rearrange("(m p) n -> p m n", p=P) for n in ("w_cmp_k1", "w_cmp_v1")]
    w_up = a["w_up"][0].rearrange("e (kt p) (h y c) -> y p e kt h c", p=P, h=2, y=2)
    w_dn = a["w_down"][0].rearrange("e (h y q p) n -> y p e h q n", p=P, q=2, y=2)
    consts = nc.inline_tensor(shape_constants(), name="shape_table").ap()

    xn2_d = nc.dram_tensor("xn2_rows", (2 * SEQ, D // 2), F32).ap()
    x2_d = nc.dram_tensor("x2_rows", (SEQ, D), F32).ap()
    moe_d = nc.dram_tensor("moe_rows", (2 * SEQ + 2 * P, D // 2), F32).ap()
    bias_d = nc.dram_tensor("bias_parts", (N_EXP, 3, 3 * D), BF16).ap()

    with ExitStack() as ctx:
        W_ALL = 53200
        arena = ctx.enter_context(nc.sbuf_tensor("arena", [P, W_ALL], F32))
        ps = ctx.enter_context(nc.psum_tensor("ps", [P, 8, 512], F32))

        def sem(name):
            return ctx.enter_context(nc.semaphore(name))

        def take(at, *shape, parts=P, dt=F32):
            n = int(np.prod(shape))
            v = arena[0:parts, at:at + (n if dt in (F32, I32, U32) else n // 2)]
            if dt != F32:
                v = v.bitcast(dt)
            if len(shape) > 1:
                names = "abcd"[:len(shape)]
                v = v.rearrange(f"p ({' '.join(names)}) -> p {' '.join(names)}",
                                **{k: s for k, s in zip(names[1:], shape[1:])})
            return v

        def bc(ap, axis, n):
            v = ap.unsqueeze(axis)
            shape = list(v.shape)
            shape[axis] = n
            return v.broadcast_to(shape)

        A_AT, B_AT, D_AT, P_AT = [0, 16384], [8192, 24576], 32768, 40960
        upw = [[take(at[par], KT, 2, 512) for at in (A_AT, B_AT)] for par in range(2)]
        dnw = take(D_AT, 2, 2, 2, D)
        stage = [take(0, NT, 512), take(2048, NT, 512)]
        xn = take(0, NT, D)
        kdup = take(4096, NT, 6, 2, HD)
        ring = [take(8192, 4096), take(12288, 4096)]
        qraw, qrot, qdil, kdil = [take(16384 + 2048 * n, 4, SEQ) for n in range(4)]
        kslc, kwin = take(24576, 2, SEQ), take(25600, 2, SEQ)
        yrows = take(26624, NT, D)
        kc = take(26624, 4, SEQ)
        blk = take(30720, 16, 4, 32)
        hT = take(32768, KT, SEQ)
        xs = take(36864, NT, D)
        gel_u, gel_t, gel_e = take(0, 256), take(256, 256), take(512, 256)
        hidT, hidv = take(768, 2, P), take(1024, 2, 2, 4, 32)
        p_cmp = take(2048, NT, 256)
        osq = take(4096, KT, SEQ)
        ygain = [take(24576, 2, D), take(30720, 2, D)]
        probs = take(26624, 4, 2, SEQ)
        oT = hT
        pcT = take(3072, 2, NT, P)
        w2k, w2v = take(7168, 2, 2, HD), take(7424, 2, HD)
        wv_half = [take(28672, 8, 256), take(4096, 8, 256)]
        bias_f = take(4096, 3 * D, parts=32)
        bias_b = take(26624, 3, 3 * D, parts=32, dt=BF16)

        cur = [P_AT]

        def put(*shape, parts=P, dt=F32):
            n = int(np.prod(shape))
            v = take(cur[0], *shape, parts=parts, dt=dt)
            cur[0] += n if dt in (F32, I32, U32) else (n + 1) // 2
            return v

        cf = put(C_ALL)
        ident = cf[:, C_ID:C_ID + P]
        identb, trib, usb, onesb = [put(P, dt=BF16) for _ in range(4)]
        mb_b = put(512, dt=BF16)
        cm_b = put(P, dt=BF16)
        ab2 = put(16)
        gbf = put(D)
        ctab = put(66, parts=1, dt=I32)
        fin = put(16)
        small_end = cur[0]
        sel = put(16, P, dt=BF16)
        xg = put(512)
        xgT = put(KT, SLOTS)
        sw_g, sw_s = put(2, 256), put(2, 256)
        sw_l, sw_t = put(256), put(256)
        act = put(2, 256)
        actT = put(2, 2, P)
        ybuf = put(512)
        biasw = put(2, 3 * D, parts=3, dt=BF16)
        rt = put(16, 6, dt=BF16)
        flatk = put(16)
        mraw, mt = put(6), put(8)
        idxg = put(1, dt=I32)
        gate_all, row_all = put(68), put(68)
        xg_in = cf[:, C_MB:C_MB + 512]
        gate_c, idxs_c = put(1), put(1, dt=I32)
        assert cur[0] <= W_ALL, cur[0]
        cur[0] = small_end
        v_slc, v_win, v_dil = put(NT, P), put(NT, P), put(NT, 512)
        pbuf = put(4, 512)
        ptb = put(3, 512)
        negm, lsum, scl = put(96), put(96), put(4, 2)
        sg = put(NT, 24)
        vt, modc, posT = put(88), put(48), put(16)
        ab1 = put(16)
        cvec, ctmp = put(KT), put(3, KT)
        posi, posf = put(NT, dt=I32), put(NT)
        ang, trig, rk = put(NT, 8), put(2, NT, 8), put(2, NT, 8)
        brow = put(32)
        st, orstd = put(6, 8), put(8)
        kcT, vc4 = put(2, 2, 32), put(2, HD)
        sc8 = put(3, 4, 8)
        wr, ones_f = put(KT, 32), put(P)
        assert cur[0] <= W_ALL - 1, cur[0]
        pT = pbuf.rearrange("p (s h) k -> p s h k", h=2)
        gbm = ptb[:, 0:2, :].rearrange("p a b -> p (a b)")
        vr = pbuf[0:88, 0, 0:P]
        cposr = pbuf[0:16, 1, 0:P]
        mrow = pbuf[:, 2:4, :]
        rope_t = ptb[:, 0:2, :].rearrange("p a (b c) -> p (a b) c", c=256)
        silu_c = ptb[:, 2, 0:KT * 32].rearrange("p (j n) -> p j n", n=32)
        zero = pbuf[:, 3, :]
        diag = pbuf[:, 0, :].rearrange("p (a b) -> p a b", b=P)
        R_AT = small_end + 2048
        lg = take(R_AT, NT, 32)
        top8, idx8 = take(R_AT + 128, NT, 8), take(R_AT + 160, NT, 8, dt=U32)
        eidx = take(R_AT + 192, NT, TOP_K)
        onehot = take(R_AT + 256, 16, 32)
        maskb = take(R_AT + 768, NT, 32, dt=BF16)
        cnt, nch = take(R_AT + 832, 32), take(R_AT + 864, 32)
        scan = [take(R_AT + 896, 48), take(R_AT + 960, 48)]
        flat_e = take(R_AT + 1024, NT, 32)
        prod = take(R_AT + 1280, 16, 32)
        gk = take(R_AT + 1792, NT, TOP_K)
        gsum = take(R_AT + 1824, NT)
        ghi = take(R_AT + 1832, 3, 16, dt=BF16)
        xn2 = yrows
        yfin, x2fin, ygain_f = take(0, NT, D), take(4096, NT, D), take(17408, NT, D)

        RING = [(("ada", n), n % 2) for n in range(4)] + [(("in", 0), 0)] + \
               [(i, 1) for i in (("ada", 4), ("ada", 5), ("in", 1))] + \
               [(i, 0) for i in (("ada", 6), ("ada", 7), ("in", 2))] + [(("in", 3), 1)] + \
               [(i, 0) for i in (("ada", 8), ("ada", 9), ("in", 4))] + \
               [(i, 1) for i in (("ada", 10), ("ada", 11), ("in", 5))] + \
               [(("c1", 0), 0), (("wo", 0), 0), (("wo", 1), 1)]
        at_ring = {item: n for n, (item, slot) in enumerate(RING)}
        IN_COLS = [(0, 512), (512, 1024), (1024, 1304), (1304, 1816), (1816, 2328), (2328, 2840)]

        def ring_view(n):
            (kind, m), slot = RING[n]
            v = ring[slot]
            if kind == "c1":
                return v.rearrange("p (m n) -> p m n", n=256)
            w = IN_COLS[m][1] - IN_COLS[m][0] if kind == "in" else 512
            return v[:, 0:KT * w].rearrange("p (k n) -> p k n", n=w)

        def before_in_slot(n):
            return [k for k in range(n) if RING[k][1] == RING[n][1]]

        units = [(ty, pr, i) for pr in range(4) for ty in (N_SLC, N_WIN) for i in range(NT)] + \
                [(N_DIL, pr, i) for pr in range(4, 8) for i in range(NT)]
        UNITS, DIL_U = len(units), 32

        def pair_end(pr):
            return 8 * (pr + 1) if pr < 4 else DIL_U + 4 * (pr - 3)

        pair_last = {pair_end(pr) - 1: pr for pr in range(8)}

        consts_in, x_in, vec_in, c_in, pos_in, brow_in, w2_in, bias_in, wr_in, wv_in = [
            sem(n) for n in ("consts_in", "x_in", "vec_in", "c_in", "pos_in", "brow_in", "w2_in", "bias_in", "wr_in",
                               "wv_in")]
        ring_in = [sem("ring_in0"), sem("ring_in1")]
        ada_ps, gb_sb, routed = [sem(n) for n in ("ada_ps", "gb_sb", "routed")]
        row_turn = sem("row_turn")
        bconst, zeroed, bias_split, bias_out = [
            sem(n) for n in ("bconst", "zeroed", "bias_split", "bias_out")]
        vt_ps, vt_sb, row_sb, modc_ps, modc_sb = [sem(n) for n in ("vt_ps", "vt_sb", "row_sb", "modc_ps", "modc_sb")]
        chain = sem("dve_chain")
        silu_e, silu_ready, trig_in, trig_ready = [sem(n) for n in ("silu_e", "silu_ready", "trig_in", "trig_ready")]
        sumsq, ms_ready, root_ready = [sem(n) for n in ("sumsq", "ms_ready", "root_ready")]
        xn_ready, tile_tr, ev_dve, ev_act = [sem(n) for n in ("xn_ready", "tile_tr", "ev_dve", "ev_act")]
        pj_ps, pj_ev, roped, tg_ps, tg_ev, ab_ready = [
            sem(n) for n in ("pj_ps", "pj_ev", "roped", "tg_ps", "tg_ev", "ab_ready")]
        blk_ready, blk_zero, hid_u, gel_in, gel_out, hid_ready, hid_tr, hid_sb, cv_ps, cv_sb = [
            sem(n) for n in ("blk_ready", "blk_zero", "hid_u", "gel_in", "gel_out", "hid_ready", "hid_tr",
                             "hid_sb", "cv_ps", "cv_sb")]
        sc_ps, sc_in, sc_exp, pc_ready, pc_tr, pc_sb = [
            sem(n) for n in ("sc_ps", "sc_in", "sc_exp", "pc_ready", "pc_tr", "pc_sb")]
        qk_done, neg_ready, exp_done, scl_ready, scaled_act, scaled_pool = [
            sem(n) for n in ("qk_done", "neg_ready", "exp_done", "scl_ready", "scaled_act", "scaled_pool")]
        tr_done, pt_dve, pt_act, pv_done, o_ev, o_sq = [
            sem(n) for n in ("tr_done", "pt_dve", "pt_act", "pv_done", "o_ev", "o_sq")]
        sq_added, osum_ps, orstd_ready, y_nsa, y_sum, yg_ready = [
            sem(n) for n in ("sq_added", "osum_ps", "orstd_ready", "y_nsa", "y_sum", "yg_ready")]
        diag_ready, diag_ps, wo_ps, x2_ready, x2_out, xn2_out, logit_ps, mask_ready, count_ps, ctab_ready = [
            sem(n) for n in ("diag_ready", "diag_ps", "wo_ps", "x2_ready", "x2_out", "xn2_out", "logit_ps",
                             "mask_ready", "count_ps", "ctab_ready")]
        gx_in, gx_out = sem("gx_in"), sem("gx_out")
        a_in, b_in = [sem("a_in0"), sem("a_in1")], [sem("b_in0"), sem("b_in1")]
        d_in = [sem("d_in0"), sem("d_in1")]
        biasw_in = [sem("biasw_in0"), sem("biasw_in1")]
        sel_ready, sel_ps, idx_ready, gathered, moved, xg_tr, xgT_ready = [
            sem(n) for n in ("sel_ready", "sel_ps", "idx_ready", "gathered", "moved", "xg_tr", "xgT_ready")]
        up_a, up_b, glu_ready, sig_ready, act_ready, act_tr, actT_ready, dn_a, dn_b, y_ready, scattered, turn = [
            sem(n) for n in ("up_a", "up_b", "glu_ready", "sig_ready", "act_ready", "act_tr", "actT_ready", "dn_a",
                             "dn_b", "y_ready", "scattered", "pool_turn")]
        fin_in = [sem(f"fin_in{i}") for i in range(NT)]
        x2_back, fin_ready, out_done, tail_chain = [sem(n) for n in ("x2_back", "fin_ready", "out_done", "tail_chain")]

        PJ = {n: NT * n for n in range(6)}
        GROUPS = [("qraw", j) for j in range(4)] + [("qrot", j) for j in range(4)] + \
                 [("dup", j) for j in range(6)] + [("kwin", j) for j in range(2)] + \
                 [("qdil", j) for j in range(4)] + [("kdil", j) for j in range(4)]
        at_group = {g: n for n, g in enumerate(GROUPS)}
        NORM_X, NORM_O, NORM_Y, NORM_H, NORM_F = range(5)
        SQ_BEFORE = [0, 4, 4, 12, 16]
        TILE_H, TILE_2 = 0, 8

        block = ctx.enter_context(nc.Block())

        @block.sync
        def _(sp):
            sp.dma_start(cf[:, :], consts[:, :]).then_inc(consts_in, 16)
            sp.dma_start(cvec[:, :], c_d.rearrange("a (p j) -> (a p) j", j=KT)).then_inc(c_in, 16)
            vecs = [("b_ada", 48), ("g_pre_mix", 8), ("g_post_mix", 8), ("g_pre_ffn", 8), ("g_post_ffn", 8),
                    ("g_out_nsa", 4), ("g_out_dil", 4)]
            row = 0
            for name, n in vecs:
                sp.dma_start(vr[row:row + n, :], a[name].rearrange("l (r q) -> (l r) q", q=P)).then_inc(vec_in, 16)
                row += n
            sp.dma_start(cposr, a["cmp_pos"][0].rearrange("(m s) d -> m (s d)", s=2)).then_inc(vec_in, 16)
            for i in range(NT):
                sp.dma_start(xs[:, i, :], x_d[i * P:(i + 1) * P, :]).then_inc(x_in, 16)
                if i == 0:
                    sp.dma_start(posi[:, :], pos_d.rearrange("a (i p) -> p (a i)", p=P),
                                 allow_slow_non_contiguous=True).then_inc(pos_in, 16)
                    sp.dma_start(brow[:, :], a["b_router"].broadcast_to([P, 32])).then_inc(brow_in, 16)

            def slot_used(n):
                kind, m = RING[n][0]
                done, count = {"ada": (ada_ps, m + 1), "in": (pj_ps, NT * (m + 1)), "c1": (hid_u, 1),
                               "wo": (wo_ps, 2 * NT * (m + 1))}[kind]
                sp.wait_ge(done, count)

            for n, ((kind, m), slot) in enumerate(RING):
                if before_in_slot(n):
                    slot_used(before_in_slot(n)[-1])
                if kind == "ada":
                    src = w_ada[:, :, m * 512:(m + 1) * 512]
                elif kind == "in":
                    src = w_in[:, :, IN_COLS[m][0]:IN_COLS[m][1]]
                elif kind == "c1":
                    src = w_c1[0]
                else:
                    src = w_o[:, :, m * 512:(m + 1) * 512]
                sp.dma_start(ring_view(n), src).then_inc(ring_in[slot], 16)
                if (kind, m) == ("in", 1):
                    for dup in range(2):
                        sp.dma_start(w2k[:, :, dup, :], a["w_cmp_k2"][0].rearrange("(j p) d -> p j d", p=P))\
                          .then_inc(w2_in, 16)
                    sp.dma_start(w2v[:, :, :], a["w_cmp_v2"][0].rearrange("(j p) d -> p j d", p=P)).then_inc(w2_in, 16)
                    sp.dma_start(wr[:, :, :], a["w_router"][0].rearrange("(k p) e -> p k e", p=P)).then_inc(wr_in, 16)
                if (kind, m) == ("in", 3):
                    sp.wait_ge(bias_out, 16)
                    sp.dma_start(wv_half[0], w_c1[1][:, 0:8, :]).then_inc(wv_in, 16)
                    sp.wait_ge(tg_ps, at_group[("dup", 5)] + 1)
                    sp.dma_start(wv_half[1], w_c1[1][:, 8:16, :]).then_inc(wv_in, 16)

            def load_up(y, par, e, dst):
                src = w_up[y][:, bass.ds(e, 1)] if not isinstance(e, int) else w_up[y][:, e:e + 1]
                for h in range(2):
                    sp.dma_start(dst[:, :, h, :], src[:, :, :, h, :].rearrange("p e k c -> p (e k) c"))\
                      .then_inc((a_in, b_in)[y][par], 16)

            def load_dn(y, e):
                src = w_dn[y][:, bass.ds(e, 1)] if not isinstance(e, int) else w_dn[y][:, e:e + 1]
                for h in range(2):
                    sp.dma_start(dnw[:, y, h], src[:, :, h].rearrange("p e q n -> p (e q) n")).then_inc(d_in[y], 16)

            def load_bias(par, e):
                src = bias_d[bass.ds(e, 1)] if not isinstance(e, int) else bias_d[e:e + 1]
                sp.dma_start(biasw[:, par, :], src.rearrange("e s n -> (e s) n")).then_inc(biasw_in[par], 16)

            sp.wait_ge(osum_ps, 1)
            load_up(0, 0, 0, upw[0][0])
            load_up(0, 1, 1, upw[1][0])
            slot_used(at_ring[("wo", 0)])
            slot_used(at_ring[("wo", 1)])
            load_up(1, 0, 0, upw[0][1])
            for i in range(NT):
                sp.wait_ge(x2_ready, i + 1)
                sp.dma_start(x2_d[i * P:(i + 1) * P, :], xs[:, i, :]).then_inc(x2_out, 16)
            for i in range(NT):
                sp.wait_ge(xn_ready, NT + i + 1)
                sp.dma_start(xn2_d[2 * i * P:2 * (i + 1) * P, :].rearrange("(p h) n -> p (h n)", h=2), xn2[:, i, :])\
                  .then_inc(xn2_out, 16)
            sp.wait_ge(x2_out, 16 * NT)
            sp.wait_ge(xn2_out, 16 * NT)
            sp.wait_ge(logit_ps, 1)
            for y in range(2):
                load_dn(y, 0)
            sp.wait_ge(routed, 1)
            sp.wait_ge(bias_out, 16)
            load_bias(0, 0)
            sp.wait_ge(gathered, 16)
            load_up(1, 1, 1, upw[1][1])
            load_bias(1, 1)

            def first_chunk(e):
                return sp.value_load(ctab[0:1, bass.ds(e + 32, 1)] if not isinstance(e, int)
                                     else ctab[0:1, e + 32:e + 33], min_val=1, max_val=64)

            def next_down(e, ends):
                sp.wait_ge(dn_a, ends)
                load_dn(0, e)
                sp.wait_ge(dn_b, ends)
                load_dn(1, e)

            with sp.Fori(1, N_EXP // 2) as e2:
                for par in range(2):
                    e = e2 * 2 + par
                    used = first_chunk(e - 1)
                    sp.wait_ge(up_a, used)
                    load_up(0, par, e, upw[par][0])
                    next_down(e - 1, used)
                    load_bias(par, e)
                    sp.wait_ge(up_b, used)
                    load_up(1, par, e, upw[par][1])
            next_down(N_EXP - 1, first_chunk(N_EXP - 1))
            total = first_chunk(N_EXP)
            sp.wait_ge(up_b, total)
            sp.dma_start(x2fin, x2_d.rearrange("(i p) n -> p i n", p=P)).then_inc(x2_back, 16)
            sp.wait_ge(scattered, total * 16 + 16)
            for i in range(NT):
                sp.dma_start(yfin[:, i, :], moe_d[2 * i * P:2 * (i + 1) * P, :].rearrange("(p h) n -> p (h n)", h=2))\
                  .then_inc(fin_in[i], 16)
            for i in range(NT):
                sp.wait_ge(fin_ready, i + 1)
                sp.dma_start(out[i * P:(i + 1) * P, :], yfin[:, i, :]).then_inc(out_done, 16)
            sp.wait_ge(out_done, 16 * NT)

        @block.gpsimd
        def _(pool):
            pool.dma_start(bias_f[:, 0:2 * D], a["b_up"][0]).then_inc(bias_in, 16)
            pool.dma_start(bias_f[:, 2 * D:3 * D], a["b_down"][0]).then_inc(bias_in, 16)
            pool.memset(onesb, 1.0).then_inc(bconst, 1)
            pool.memset(ones_f, 1.0).then_inc(bconst, 1)
            pool.wait_ge(consts_in, 16)
            for dst, at, n in ((identb, C_ID, P), (trib, C_TRI, P), (usb, C_US, P), (mb_b, C_MB, 512), (cm_b, C_CM, P)):
                pool.tensor_copy(dst, cf[:, at:at + n]).then_inc(bconst, 1)
            pool.wait_ge(bias_in, 32)
            for part in range(3):
                pool.tensor_copy(bias_b[:, part, :], bias_f[:, :]).then_inc(bias_split, 1)
                pool.wait_ge(bias_split, 2 * part + 1)
                if part < 2:
                    pool.tensor_tensor(bias_f[:, :], bias_f[:, :], bias_b[:, part, :], ALU.subtract)\
                        .then_inc(bias_split, 1)
                    pool.wait_ge(bias_split, 2 * part + 2)
            pool.dma_start(bias_d, bias_b).then_inc(bias_out, 16)
            pool.wait_ge(bias_out, 16)
            pool.memset(blk[:, :, :, 31:32], 0.0).then_inc(blk_zero, 1)

            def add_squares(pr):
                if pr % 4:
                    dst = osq[:, pr // 4 * 4, :]
                    pool.wait_ge(o_sq, pr + 1)
                    pool.tensor_tensor(dst, dst, osq[:, pr, :], ALU.add).then_inc(sq_added, 1)
                    pool.wait_ge(sq_added, pr - pr // 4)

            for u, (ty, pr, i) in enumerate(units):
                pb = probs[:, u % 4, 1, 0:P * (i + 1)]
                pool.wait_ge(scl_ready, u + 1)
                pool.tensor_scalar(pb, pb, scl[:, u % 4, 1:2], None, ALU.mult).then_inc(scaled_pool, 1)
                if u - 6 in pair_last:
                    add_squares(pair_last[u - 6])
            add_squares(6)
            add_squares(7)
            pool.wait_ge(pv_done, UNITS)
            pool.memset(zero, 0.0).then_inc(zeroed, 1)
            pool.wait_ge(zeroed, 1)
            pool.dma_start(moe_d.rearrange("(r p) n -> p r n", p=P), bc(zero, 1, (2 * SEQ + 2 * P) // P))\
                .then_inc(scattered, 16)
            pool.wait_ge(scattered, 16)
            pool.wait_ge(xn2_out, 16 * NT)

            def gather():
                pool.indirect_dma_start(xg_in, None, xn2_d, bass.IndirectOffsetOnAxis(idxg, 0)).then_inc(gathered, 16)

            pool.wait_ge(idx_ready, 1)
            gather()
            pool.wait_ge(gathered, 16)
            pool.tensor_copy(xg, xg_in).then_inc(moved, 1)
            pool.wait_ge(moved, 1)
            pool.wait_ge(idx_ready, 2)
            gather()
            pool.wait_ge(ctab_ready, 1)
            total = pool.value_load(ctab[0:1, 64:65], min_val=1, max_val=64)
            with pool.Fori(0, total) as c:
                pool.wait_ge(gathered, c * 16 + 32)
                pool.wait_ge(xg_tr, c + 1)
                pool.sem_inc(turn, 1)
                pool.tensor_copy(xg, xg_in).then_inc(moved, 1)
                pool.wait_ge(idx_ready, c + 3)
                pool.wait_ge(moved, c + 2)
                pool.sem_inc(turn, 1)
                gather()
                pool.wait_ge(y_ready, c + 1)
                pool.wait_ge(scattered, c * 16 + 16)
                pool.sem_inc(turn, 1)
                pool.indirect_dma_start(moe_d, bass.IndirectOffsetOnAxis(idxs_c, 0), ybuf, None,
                                        compute_op=ALU.add).then_inc(scattered, 16)

        @block.scalar
        def _(act_e):
            def root(norm):
                act_e.wait_ge(ms_ready, norm + 1)
                act_e.activation(st[:, 2, :], st[:, 1, :], ACT.Sqrt).then_inc(root_ready, 1)
                if norm == NORM_O:
                    act_e.wait_ge(orstd_ready, 1)

            junk = pbuf[:, 1, :]

            def square(src, col, before):
                act_e.activation(junk, src, ACT.Square, accum_out=st[:, 0, col:col + 1]).then_inc(sumsq, 1)
                act_e.wait_ge(sumsq, before + 1)

            act_e.wait_ge(c_in, 16)
            act_e.activation(ctmp[:, 0, :], cvec, ACT.Exp, scale=-1.0).then_inc(silu_e, 1)
            act_e.wait_ge(trig_in, 1)
            act_e.activation(trig, rk, ACT.Sin).then_inc(trig_ready, 1)
            act_e.wait_ge(x_in, 16 * NT)
            for i in range(NT):
                act_e.activation(xn[:, i, :], xs[:, i, :], ACT.Square, accum_out=st[:, 0, i:i + 1])\
                    .then_inc(sumsq, 1)
            root(NORM_X)

            def tile_evac(base, dst, ab):
                for kt in range(1, KT, 2):
                    act_e.wait_ge(tile_tr, base + kt + 1)
                    act_e.activation(dst[:, kt, :], ps[:, kt % 4, :], ACT.Identity, bias=ab[1][:, kt:kt + 1] if ab[1]
                                     is not None else 0.0, scale=ab[0][:, kt:kt + 1]).then_inc(ev_act, 1)

            act_e.wait_ge(ab_ready, 1)
            tile_evac(TILE_H, hT, (ab1[:, 0:8], ab1[:, 8:16]))

            def proj_evac(n):
                for i in range(NT):
                    t = PJ[n] + i
                    b = ps[:, t % 2, :]
                    if n == 5:
                        gelu(i)
                    act_e.wait_ge(pj_ps, t + 1)
                    if n == 0 or n == 3 or n == 4:
                        if i == 0 and n == 3:
                            act_e.wait_ge(tg_ps, at_group[("qrot", 3)] + 1)
                        if i == 0 and n == 4:
                            act_e.wait_ge(tg_ps, at_group[("kwin", 1)] + 1)
                        act_e.activation(stage[1 if n == 4 else 0][:, i, :], b, ACT.Copy).then_inc(pj_ev, 1)
                    elif n == 1:
                        if i == 0:
                            act_e.wait_ge(bias_split, 5)
                        for dup in range(2):
                            act_e.activation(kdup[:, i, :, dup, :], b[:, 0:384].rearrange("p (g d) -> p g d", d=HD),
                                             ACT.Copy)
                        act_e.activation(v_slc[:, i, :], b[:, 384:512], ACT.Copy).then_inc(pj_ev, 1)
                    elif n == 2:
                        for dup in range(2):
                            act_e.activation(
                                stage[1][:, i, 0:256].rearrange("p (g u d) -> p g u d", g=2, u=2)[:, :, dup, :],
                                b[:, 0:128].rearrange("p (g d) -> p g d", d=HD), ACT.Copy)
                        act_e.activation(v_win[:, i, :], b[:, 128:256], ACT.Copy)
                        act_e.activation(sg[:, i, :], b[:, 256:280], ACT.Exp, scale=-1.0).then_inc(pj_ev, 1)
                    else:
                        act_e.activation(v_dil[:, i, :], b, ACT.Copy).then_inc(pj_ev, 1)

            def gelu(i):
                if i == 2:
                    act_e.wait_ge(hid_u, 1)
                    act_e.activation(gel_u, ps[:, 3, 0:256], ACT.Copy).then_inc(gel_in, 1)
                    act_e.wait_ge(gel_in, 2)
                    act_e.activation(gel_e, gel_t, ACT.Exp, scale=-2.0 * float(np.sqrt(2.0 / np.pi)))\
                        .then_inc(gel_out, 1)

            for n in range(6):
                proj_evac(n)
            act_e.wait_ge(sc_in, 1)
            act_e.activation(p_cmp, p_cmp, ACT.Exp).then_inc(sc_exp, 1)

            def exps(u):
                ty, pr, i = units[u]
                w = P * (i + 1)
                act_e.wait_ge(neg_ready, u + 1)
                if u >= 4:
                    act_e.wait_ge(tr_done, u - 3)
                for h in range(2):
                    n = 2 * u + h
                    ins = act_e.activation(probs[:, u % 4, h, 0:w], ps[:, u % 2 * 2 + h, 0:w], ACT.Exp,
                                           bias=negm[:, n:n + 1],
                                           accum_out=lsum[:, n:n + 1] if ty != N_DIL else None)
                ins.then_inc(exp_done, 1)

            def scale_first(u):
                act_e.wait_ge(scl_ready, u + 1)
                pb = probs[:, u % 4, 0, 0:P * (units[u][2] + 1)]
                act_e.activation(pb, pb, ACT.Copy, scale=scl[:, u % 4, 0:1]).then_inc(scaled_act, 1)

            def pair_squares(pr):
                act_e.wait_ge(o_ev, pr + 1)
                act_e.activation(osq[:, pr, :], ps[:, 6 + pr % 2, :], ACT.Square).then_inc(o_sq, 1)

            exps(0)
            exps(1)
            scale_first(0)
            exps(2)
            scale_first(1)
            for u, (ty, pr, i) in enumerate(units):
                if ty == N_DIL:
                    w = P * (i + 1)
                    act_e.wait_ge(tr_done, u + 1)
                    act_e.wait_ge(pv_done, u - 1)
                    act_e.activation(pT[:, u % 2, :, 0:w], ps[:, 4:6, 0:w], ACT.Copy).then_inc(pt_act, 1)
                if u + 2 < UNITS:
                    scale_first(u + 2)
                if u + 3 < UNITS:
                    exps(u + 3)
                if u - 2 in pair_last:
                    pair_squares(pair_last[u - 2])
            pair_squares(7)

            root(NORM_O)
            for n in range(2):
                for i in range(NT):
                    act_e.wait_ge(wo_ps, 8 * n + i + 1)
                    act_e.activation(yrows[:, i, 512 * n:512 * (n + 1)], ps[:, i, :], ACT.Copy,
                                     scale=orstd[:, i:i + 1]).then_inc(y_nsa, 1)
            for n in range(2):
                for i in range(NT):
                    act_e.wait_ge(y_sum, 4 * n + i + 1)
                    square(yrows[:, i, 512 * n:512 * (n + 1)], 4 * n + i, SQ_BEFORE[NORM_Y] + 4 * n + i)
            root(NORM_Y)
            for i in range(NT):
                act_e.wait_ge(x2_ready, i + 1)
                act_e.activation(xn2[:, i, :], xs[:, i, :], ACT.Square, accum_out=st[:, 0, i:i + 1]).then_inc(sumsq, 1)
            root(NORM_H)
            act_e.wait_ge(ab_ready, 2)
            tile_evac(TILE_2, hT, (ab2[:, 0:8], ab2[:, 8:16]))
            act_e.wait_ge(gx_in, 1)
            act_e.activation(gk, gk, ACT.Exp).then_inc(gx_out, 1)

            def spread(turns):
                act_e.wait_ge(xg_tr, turns)
                for kt in range(KT):
                    src = ps[:, 2, (kt % 4) * P + (kt // 4) * SLOTS:(kt % 4) * P + (kt // 4) * SLOTS + SLOTS]
                    ins = act_e.activation(xgT[:, kt, :], src, ACT.Identity, bias=ab2[:, 8 + kt:9 + kt],
                                           scale=ab2[:, kt:kt + 1])
                ins.then_inc(xgT_ready, 1)

            spread(1)
            act_e.wait_ge(ctab_ready, 1)
            total = act_e.value_load(ctab[0:1, 64:65], min_val=1, max_val=64)
            with act_e.Fori(0, total) as c:
                act_e.wait_ge(glu_ready, c * 2 + 1)
                act_e.activation(sw_s[:, 0], sw_g[:, 0], ACT.Sigmoid, scale=ALPHA).then_inc(sig_ready, 1)
                act_e.wait_ge(glu_ready, c * 2 + 2)
                act_e.activation(sw_s[:, 1], sw_g[:, 1], ACT.Sigmoid, scale=ALPHA).then_inc(sig_ready, 1)
                spread(c + 2)
            for i in range(NT):
                act_e.wait_ge(fin_in[i], 16)
                act_e.activation(take(16384, D), yfin[:, i, :], ACT.Square, accum_out=fin[:, i:i + 1])\
                    .then_inc(sumsq, 1)
                act_e.wait_ge(sumsq, SQ_BEFORE[NORM_F] + i + 1)
            act_e.wait_ge(ms_ready, NORM_F + 1)
            act_e.activation(fin[:, 8:12], fin[:, 4:8], ACT.Sqrt).then_inc(root_ready, 1)

        @block.vector
        def _(v):
            links = [0]

            def link(ins):
                links[0] += 1
                ins.then_inc(chain, 1)
                v.wait_ge(chain, links[0])

            def rstd(norm, n, width):
                ss, ms, rt_, r, t = [st[:, row, 0:n] for row in range(5)]
                v.wait_ge(sumsq, SQ_BEFORE[norm + 1])
                if norm == NORM_Y:
                    link(v.tensor_tensor(ss, ss, st[:, 0, n:2 * n], ALU.add))
                v.tensor_scalar(ms, ss, 1.0 / width, EPS, ALU.mult, ALU.add).then_inc(ms_ready, 1)
                v.wait_ge(root_ready, norm + 1)
                link(v.reciprocal(r, rt_))
                link(v.tensor_tensor(t, r, r, ALU.mult))
                link(v.tensor_tensor(t, t, ms, ALU.mult))
                link(v.tensor_scalar(t, t, -0.5, 1.5, ALU.mult, ALU.add))
                link(v.tensor_tensor(r, r, t, ALU.mult))

            link(v.memset(kcT, 0.0))
            link(v.memset(st[:, :, :], 1.0))
            v.wait_ge(silu_e, 1)
            link(v.tensor_scalar(ctmp[:, 1, :], ctmp[:, 0, :], 1.0, None, ALU.add))
            link(v.reciprocal(ctmp[:, 2, :], ctmp[:, 1, :]))
            link(v.tensor_tensor(cvec, cvec, ctmp[:, 2, :], ALU.mult))
            v.tensor_copy(silu_c, bc(cvec, 2, 32)).then_inc(silu_ready, 1)
            v.wait_ge(pos_in, 16)
            v.wait_ge(consts_in, 16)
            link(v.tensor_copy(posf, posi))
            link(v.tensor_tensor(ang, bc(posf, 2, 8), bc(cf[:, C_INVF:C_INVF + 8], 1, NT), ALU.mult))
            C1, C2 = 6.28125, 0.00193500518798828125
            C3 = 2.0 * np.pi - C1 - C2
            for w, quarter in ((0, 0.0), (1, 0.25)):
                k = rk[:, w]
                link(v.tensor_scalar(k, ang, 1.0 / (2.0 * np.pi), quarter, ALU.mult, ALU.add))
                link(v.tensor_scalar(k, k, MAGIC, MAGIC, ALU.add, ALU.subtract))
                r = trig[:, w]
                link(v.scalar_tensor_tensor(out=r, in0=k, scalar=-C1, in1=ang, op0=ALU.mult, op1=ALU.add))
                link(v.scalar_tensor_tensor(out=r, in0=k, scalar=-C2, in1=r, op0=ALU.mult, op1=ALU.add))
                link(v.scalar_tensor_tensor(out=r, in0=k, scalar=-C3, in1=r, op0=ALU.mult, op1=ALU.add))
                link(v.tensor_scalar(r, r, quarter * 2.0 * np.pi, 3.1415925, ALU.add, ALU.min))
                ins = v.tensor_scalar(k, r, -3.1415925, None, ALU.max)
                if w == 0:
                    link(ins)
                else:
                    ins.then_inc(trig_in, 1)
            v.wait_ge(vt_ps, 1)
            link(v.tensor_copy(vt, ps[:, 7, 0:88]))
            v.tensor_copy(posT, ps[:, 7, 128:144]).then_inc(vt_sb, 1)
            rstd(NORM_X, 4, D)
            for i in range(NT):
                v.tensor_scalar(xn[:, i, :], xs[:, i, :], st[:, 3, i:i + 1], None, ALU.mult).then_inc(xn_ready, 1)

            def ada_rows(n):
                v.wait_ge(ada_ps, n + 1)
                if n >= 2:
                    v.wait_ge(modc_ps, n - 1)
                v.tensor_copy(mrow[:, n % 2, :], ps[:, 2, :]).then_inc(row_sb, 1)

            def ada_cols(lo, hi):
                v.wait_ge(modc_ps, hi)
                v.tensor_tensor(modc[:, 4 * lo:4 * hi], ps[:, 3, 4 * lo:4 * hi], vt[:, 4 * lo:4 * hi], ALU.add)\
                    .then_inc(modc_sb, 1)

            for n in range(4):
                ada_rows(n)
            ada_cols(0, 4)
            v.wait_ge(modc_sb, 1)
            link(v.scalar_tensor_tensor(out=ab1[:, 0:8], in0=modc[:, 8:16], scalar=1.0, in1=vt[:, 48:56],
                                        op0=ALU.add, op1=ALU.mult))
            v.tensor_copy(ab1[:, 8:16], modc[:, 0:8]).then_inc(ab_ready, 1)
            v.wait_ge(ab_ready, 1)

            def tile_evac(base, dst, ab):
                for kt in range(0, KT, 2):
                    v.wait_ge(tile_tr, base + kt + 1)
                    v.tensor_scalar(dst[:, kt, :], ps[:, kt % 4, :], ab[0][:, kt:kt + 1],
                                    ab[1][:, kt:kt + 1] if ab[1] is not None else None, ALU.mult,
                                    ALU.add if ab[1] is not None else ALU.bypass).then_inc(ev_dve, 1)

            tile_evac(TILE_H, hT, (ab1[:, 0:8], ab1[:, 8:16]))
            v.wait_ge(trig_ready, 1)

            def rope(view, n, heads_n):
                x1, x2 = view[:, :, :, 0:8], view[:, :, :, 8:16]
                cos, sin = bc(trig[:, 1], 2, heads_n), bc(trig[:, 0], 2, heads_n)
                tb = [rope_t[:, m, 0:NT * heads_n * 8].rearrange("p (i h d) -> p i h d", i=NT, h=heads_n)
                      for m in range(4)]
                for dst, src, w in ((0, x1, cos), (1, x2, sin), (2, x2, cos), (3, x1, sin)):
                    ins = v.tensor_tensor(tb[dst], src, w, ALU.mult)
                link(ins)
                v.tensor_tensor(x1, tb[0], tb[1], ALU.subtract)
                v.tensor_tensor(x2, tb[2], tb[3], ALU.add).then_inc(roped, 1)
                v.wait_ge(roped, n)

            def group_evac(g):
                kind, j = GROUPS[g]
                v.wait_ge(tg_ps, g + 1)
                b = ps[:, 4 + g % 4, :]
                if kind in ("qraw", "qrot", "qdil"):
                    dst = {"qraw": qraw, "qrot": qrot, "qdil": qdil}[kind][:, j, :]
                    v.tensor_scalar(dst, b, HD ** -0.5, None, ALU.mult).then_inc(tg_ev, 1)
                elif kind == "dup" and j < 4:
                    if j == 0:
                        v.wait_ge(bias_out, 16)
                    v.tensor_copy(kc[0:HD, j, :], b[0:HD, :])
                    v.tensor_copy(kc[HD:P, j, 0:SEQ - 1], b[HD:P, 1:SEQ]).then_inc(tg_ev, 1)
                else:
                    dst = kslc[:, j - 4, :] if kind == "dup" else kwin[:, j, :] if kind == "kwin" else kdil[:, j, :]
                    v.tensor_copy(dst, b).then_inc(tg_ev, 1)

            def heads_of(buf):
                return buf.rearrange("p i (h d) -> p i h d", d=HD)

            def gain_rows(m, half, n):
                if n:
                    v.wait_ge(diag_ps, n)
                for q in range(4):
                    kt = 4 * half + q
                    col = (16, 40)[m] + kt
                    ins = v.tensor_scalar(diag[:, q, :], ident, modc[:, col:col + 1], None, ALU.mult)
                ins.then_inc(diag_ready, 1)
                v.wait_ge(diag_ps, n + 1)
                v.tensor_copy((gbm, gbf)[m][:, half * 512:(half + 1) * 512], ps[:, 2, :]).then_inc(gb_sb, 1)
                v.wait_ge(gb_sb, n + 1)

            for n in range(4, 8):
                ada_rows(n)
            for g in range(0, 4):
                group_evac(g)
            rope(heads_of(stage[0]), 1, 8)
            v.wait_ge(pj_ev, PJ[1] + NT)
            rope(kdup[:, :, 4:6].rearrange("p i g u d -> p i (g u) d"), 2, 4)
            for g in range(4, 14):
                group_evac(g)
            v.wait_ge(tg_ev, 14)
            v.wait_ge(blk_zero, 1)
            v.wait_ge(vt_sb, 1)
            for q in range(4):
                src = bass.AP(kc.tensor, kc.offset + q * SEQ, [[kc.ap[0][0], P], [2, 16], [16, 31]])
                ins = v.tensor_tensor(blk[:, :, q, 0:31], src, bc(posT, 2, 31), ALU.add)
            ins.then_inc(blk_ready, 1)
            v.wait_ge(pj_ev, PJ[2] + NT)
            rope(heads_of(stage[1][:, :, 0:256]), 3, 4)
            for n in range(8, 10):
                ada_rows(n)
            for g in range(14, 16):
                group_evac(g)
            v.wait_ge(pj_ev, PJ[3] + NT)
            rope(heads_of(stage[0]), 4, 8)
            for n in range(10, 12):
                ada_rows(n)
            ada_cols(4, 12)
            v.wait_ge(modc_sb, 2)
            link(v.scalar_tensor_tensor(out=ab2[:, 0:8], in0=modc[:, 32:40], scalar=1.0, in1=vt[:, 64:72],
                                        op0=ALU.add, op1=ALU.mult))
            v.tensor_copy(ab2[:, 8:16], modc[:, 24:32]).then_inc(ab_ready, 1)
            link(v.tensor_tensor(modc[:, 16:24], modc[:, 16:24], vt[:, 56:64], ALU.mult))
            link(v.tensor_tensor(modc[:, 40:48], modc[:, 40:48], vt[:, 72:80], ALU.mult))
            for g in range(16, 20):
                group_evac(g)
            for half in range(2):
                gain_rows(1, half, half)
            v.wait_ge(pj_ev, PJ[4] + NT)
            rope(heads_of(stage[1]), 5, 8)
            link(v.tensor_scalar(sg, sg, 1.0, None, ALU.add))
            link(v.reciprocal(sg, sg))
            v.wait_ge(gel_in, 1)
            link(v.tensor_tensor(gel_t, gel_u, gel_u, ALU.mult))
            link(v.tensor_scalar(gel_t, gel_t, 0.044715, 1.0, ALU.mult, ALU.add))
            v.tensor_tensor(gel_t, gel_t, gel_u, ALU.mult).then_inc(gel_in, 1)
            v.wait_ge(gel_out, 1)
            link(v.tensor_scalar(gel_e, gel_e, 1.0, None, ALU.add))
            link(v.reciprocal(gel_e, gel_e))
            v.tensor_tensor(gel_u, gel_u, gel_e, ALU.mult).then_inc(hid_ready, 1)
            v.wait_ge(hid_tr, 1)
            hps = ps[:, 2, 0:256].rearrange("p (j q) -> p j q", j=2)
            v.tensor_copy(hidT, hps)
            for g in range(2):
                src = bc(hps[:, :, 64 + 32 * g:96 + 32 * g], 2, 4)
                ins = v.tensor_copy(hidv[:, :, g], src)
            ins.then_inc(hid_sb, 1)
            v.wait_ge(cv_ps, 1)
            for u in range(2):
                rows = slice(64 * u, 64 * u + 64)
                v.tensor_copy(kcT[rows, :, u, :], ps[rows, 3, 0:64].rearrange("p (g c) -> p g c", g=2))
            v.tensor_copy(vc4, ps[:, 3, 64:192].rearrange("p (g d) -> p g d", g=2)).then_inc(cv_sb, 1)
            for g in range(20, 24):
                group_evac(g)
            for half in range(2):
                gain_rows(0, half, 2 + half)
            v.wait_ge(sc_ps, 1)
            s_view = ps[:, 4:6, :].rearrange("p b (i h c) -> p (b i h) c", h=8, c=32)
            p_view = p_cmp.rearrange("p i (h c) -> p (i h) c", c=32)
            m32, l32, g32 = [sc8[:, m].rearrange("p i h -> p (i h)") for m in range(3)]
            link(v.tensor_reduce(m32, s_view, AX.X, ALU.max, negate=True))
            v.tensor_tensor(p_view, s_view, bc(m32, 2, 32), ALU.add).then_inc(sc_in, 1)

            def row_max(u):
                w = P * (units[u][2] + 1)
                b = u % 2 * 2
                v.wait_ge(qk_done, u + 1)
                v.tensor_reduce(negm[:, 2 * u:2 * u + 2], ps[:, b:b + 2, 0:w], AX.X, ALU.max, negate=True)\
                    .then_inc(neg_ready, 1)

            def sums(u):
                ty, pr, i = units[u]
                v.wait_ge(exp_done, u + 1)
                ls = lsum[:, 2 * u:2 * u + 2]
                if ty == N_DIL:
                    for h in range(2):
                        pb = probs[:, u % 4, h, 0:P * (i + 1)]
                        ins = v.tensor_tensor_reduce(pb, pb, cf[:, C_MULT + (3 - i) * P:C_MULT + 512], 1.0, 0.0,
                                                     ALU.mult, ALU.add, lsum[:, 2 * u + h:2 * u + h + 1])
                    link(ins)
                if u >= 4:
                    v.wait_ge(scaled_pool, u - 3)
                    v.wait_ge(scaled_act, u - 3)
                dst = scl[:, u % 4, :]
                if ty == N_DIL:
                    v.reciprocal(dst, ls).then_inc(scl_ready, 1)
                else:
                    link(v.reciprocal(dst, ls))
                    v.tensor_tensor(dst, dst, sg4[:, i, 2 * pr:2 * pr + 2, ty + 1], ALU.mult).then_inc(scl_ready, 1)

            def pt_evac(u):
                ty, pr, i = units[u]
                if ty == N_DIL:
                    return
                w = P * (i + 1)
                v.wait_ge(tr_done, u + 1)
                if u >= 2:
                    v.wait_ge(pv_done, u - 1)
                v.tensor_copy(pT[:, u % 2, :, 0:w], ps[:, 4:6, 0:w]).then_inc(pt_dve, 1)

            def pair_out(pr):
                v.wait_ge(pv_done, pair_end(pr))
                v.tensor_scalar(oT[:, pr, :], ps[:, 6 + pr % 2, :], vt[:, 80 + pr:81 + pr], None, ALU.mult)\
                    .then_inc(o_ev, 1)

            def compressed_probs():
                v.wait_ge(sc_exp, 1)
                link(v.tensor_reduce(l32, p_view, AX.X, ALU.add))
                link(v.reciprocal(l32, l32))
                link(v.tensor_tensor(sc8[:, 2], sc8[:, 1], sg4[:, :, :, 0], ALU.mult))
                link(v.tensor_tensor(p_view, p_view, bc(g32, 2, 32), ALU.mult))
                valid = cf[:, C_CV:C_CV + P].rearrange("p (i c) -> p i c", c=32)
                p4 = p_cmp.rearrange("p i (h c) -> p i h c", c=32)
                v.tensor_tensor(p4, p4, bc(valid, 2, 8), ALU.mult).then_inc(pc_ready, 1)

            def compressed_evac(g):
                v.wait_ge(pc_tr, g + 1)
                v.tensor_copy(pcT[:, g], ps[:, 7, :].rearrange("p (i q) -> p i q", i=NT)).then_inc(pc_sb, 1)

            sg4 = sg.rearrange("p i (h t) -> p i h t", t=3)
            row_max(0)
            row_max(1)
            sums(0)
            row_max(2)
            compressed_probs()
            sums(1)
            for u in range(UNITS):
                pt_evac(u)
                if u in (1, 2):
                    compressed_evac(u - 1)
                if u + 2 < UNITS:
                    sums(u + 2)
                if u + 3 < UNITS:
                    row_max(u + 3)
                if u - 2 in pair_last:
                    pair_out(pair_last[u - 2])
            pair_out(7)

            v.wait_ge(osum_ps, 1)
            link(v.tensor_copy(st[:, 0, :], ps[:, 7, 0:8]))
            rstd(NORM_O, 8, 512)
            v.tensor_copy(orstd, st[:, 3, :]).then_inc(orstd_ready, 1)
            v.wait_ge(orstd_ready, 1)
            for n in range(2):
                for i in range(NT):
                    v.wait_ge(wo_ps, 8 * n + 4 + i + 1)
                    v.wait_ge(y_nsa, 4 * n + i + 1)
                    y = yrows[:, i, 512 * n:512 * (n + 1)]
                    v.scalar_tensor_tensor(out=y, in0=ps[:, 4 + i, :], scalar=orstd[:, 4 + i:5 + i], in1=y,
                                           op0=ALU.mult, op1=ALU.add).then_inc(y_sum, 1)
                    v.wait_ge(y_sum, 4 * n + i + 1)
                    v.tensor_tensor(ygain[i // 2][:, i % 2, 512 * n:512 * (n + 1)], y,
                                    gbm[:, 512 * n:512 * (n + 1)], ALU.mult).then_inc(yg_ready, 1)
            rstd(NORM_Y, 4, D)
            v.wait_ge(yg_ready, 2 * NT)
            for i in range(NT):
                v.scalar_tensor_tensor(out=xs[:, i, :], in0=ygain[i // 2][:, i % 2, :], scalar=st[:, 3, i:i + 1],
                                       in1=xs[:, i, :], op0=ALU.mult, op1=ALU.add).then_inc(x2_ready, 1)
            v.wait_ge(x2_ready, NT)
            rstd(NORM_H, 4, D)
            for i in range(NT):
                v.tensor_scalar(xn2[:, i, :], xs[:, i, :], st[:, 3, i:i + 1], None, ALU.mult).then_inc(xn_ready, 1)
            tile_evac(TILE_2, hT, (ab2[:, 0:8], ab2[:, 8:16]))

            v.wait_ge(logit_ps, 1)
            v.wait_ge(brow_in, 16)
            link(v.tensor_tensor(lg, ps[:, 4, 0:P].rearrange("p (i e) -> p i e", e=32), bc(brow, 1, NT), ALU.add))
            for i in range(NT):
                ins = v.max(top8[:, i, :], lg[:, i, :])
            link(ins)
            for i in range(NT):
                ins = v.max_index(idx8[:, i, :], top8[:, i, :], lg[:, i, :])
            link(ins)
            v.tensor_tensor(gk, top8[:, :, 0:TOP_K], top8[:, :, 0:1].broadcast_to([P, NT, TOP_K]), ALU.subtract)\
                .then_inc(gx_in, 1)
            link(v.tensor_copy(eidx, idx8[:, :, 0:TOP_K]))
            link(v.tensor_tensor(onehot, bc(cf[:, C_I32:C_I32 + 32], 1, 16),
                                 bc(eidx.rearrange("p i k -> p (i k)"), 2, 32), ALU.is_equal))
            oh4 = onehot.rearrange("p (i k) e -> p i k e", k=TOP_K)
            with nc.allow_low_precision("sums of zeros and ones are exact"):
                v.tensor_reduce(maskb, onehot.rearrange("p (i k) e -> p i e k", k=TOP_K), AX.X, ALU.add)\
                    .then_inc(mask_ready, 1)
            v.wait_ge(count_ps, 1)
            link(v.tensor_scalar(cnt, ps[:, 6, 0:32], 1.0 / SLOTS, (SLOTS - 1.0) / SLOTS - 0.5 + 0.5 / SLOTS,
                                 ALU.mult, ALU.add))
            link(v.tensor_scalar(nch, cnt, MAGIC, MAGIC, ALU.add, ALU.subtract))
            link(v.tensor_scalar(nch, nch, 1.0, None, ALU.max))
            v.memset(scan[0][:, 0:16], 0.0)
            v.memset(scan[1][:, 0:16], 0.0)
            link(v.tensor_copy(scan[0][:, 16:48], nch))
            for s in range(5):
                src, dst = scan[s % 2], scan[(s + 1) % 2]
                link(v.tensor_tensor(dst[:, 16:48], src[:, 16:48], src[:, 16 - (1 << s):48 - (1 << s)], ALU.add))
            last = scan[1]
            v.tensor_copy(ctab[0:1, 64:65], last[0:1, 47:48])
            v.tensor_copy(ctab[0:1, 0:32], nch[0:1, :])
            link(v.tensor_tensor(cnt, last[:, 16:48], nch, ALU.subtract))
            v.tensor_copy(ctab[0:1, 32:64], cnt[0:1, :]).then_inc(ctab_ready, 1)
            v.wait_ge(ctab_ready, 1)
            link(v.tensor_scalar(cnt, cnt, float(SLOTS), None, ALU.mult))
            link(v.tensor_tensor(flat_e, ps[:, 5, 0:P].rearrange("p (i e) -> p i e", e=32), bc(cnt, 1, NT), ALU.add))
            link(v.tensor_tensor(prod.rearrange("p (i k) e -> p i k e", k=TOP_K), oh4, bc(flat_e, 2, TOP_K), ALU.mult))
            link(v.tensor_reduce(flatk, prod, AX.X, ALU.add))
            v.wait_ge(gx_out, 1)
            link(v.tensor_reduce(gsum, gk, AX.X, ALU.add))
            link(v.reciprocal(gsum, gsum))
            link(v.tensor_tensor(gk, gk, bc(gsum, 2, TOP_K), ALU.mult))
            gflat = gk.rearrange("p i k -> p (i k)")
            for part in range(3):
                link(v.tensor_copy(ghi[:, part], gflat))
                v.tensor_copy(rt[:, :, 3 + part], ghi[:, part])
                if part < 2:
                    link(v.tensor_tensor(gflat, gflat, ghi[:, part], ALU.subtract))
            v.tensor_copy(rt[:, :, 0:3], cf[:, C_RT:C_RT + 48].rearrange("p (n c) -> p n c", c=3)).then_inc(routed, 1)

            iota_b = bc(cf[:, C_IOTA:C_IOTA + P], 1, 16)

            def pick():
                v.tensor_tensor(sel, iota_b, bc(flatk, 2, P), ALU.is_equal).then_inc(sel_ready, 1)

            pick()
            v.wait_ge(sel_ready, 1)
            link(v.tensor_scalar(flatk, flatk, float(SLOTS), None, ALU.subtract))

            def indices(step, m):
                step(v.tensor_copy(mraw, ps[:, 6, 0:6]))
                v.tensor_tensor(mt[:, 1:2], mraw[:, 3:4], mraw[:, 4:5], ALU.add)
                step(v.tensor_tensor(mt[:, 0:1], mraw[:, 0:1], mraw[:, 1:2], ALU.add))
                v.tensor_tensor(gate_all[:, m], mt[:, 1:2], mraw[:, 5:6], ALU.add)
                v.tensor_scalar(idxg, mt[:, 0:1], 2.0, cf[:, C_HALF:C_HALF + 1], ALU.mult, ALU.add)
                step(v.tensor_scalar(mt[:, 2:3], mt[:, 0:1], 2.0, cf[:, C_PADH:C_PADH + 1], ALU.mult, ALU.add))
                v.scalar_tensor_tensor(out=row_all[:, m], in0=mraw[:, 2:3], scalar=cf[:, C_NEGP:C_NEGP + 1],
                                       in1=mt[:, 2:3], op0=ALU.mult, op1=ALU.add).then_inc(idx_ready, 1)

            for m in range(2):
                v.wait_ge(sel_ps, m + 1)
                if m:
                    v.wait_ge(gathered, 16)
                indices(link, slice(m, m + 1))
                pick()
                v.wait_ge(sel_ready, m + 2)
                if m == 0:
                    link(v.tensor_scalar(flatk, flatk, float(SLOTS), None, ALU.subtract))
            v.wait_ge(ctab_ready, 1)
            total = v.value_load(ctab[0:1, 64:65], min_val=1, max_val=64)
            BASE = links[0]
            PER = 9
            with v.Fori(0, total) as c:
                n_in = [0]
                base = v.snap(c * PER + BASE)

                def step(ins):
                    n_in[0] += 1
                    ins.then_inc(chain, 1)
                    v.wait_ge(chain, base + n_in[0])

                def glu(y):
                    up = ps[:, y, :].rearrange("p (n two) -> p n two", two=2)
                    v.wait_ge((up_a, up_b)[y], c + 1)
                    v.tensor_scalar(sw_g[:, y], up[:, :, 0], LIMIT, None, ALU.min).then_inc(glu_ready, 1)
                    step(v.tensor_scalar(sw_l, up[:, :, 1], LIMIT, -LIMIT, ALU.min, ALU.max))
                    v.wait_ge(glu_ready, c * 2 + y + 1)
                    step(v.scalar_tensor_tensor(out=sw_t, in0=sw_l, scalar=1.0, in1=sw_g[:, y], op0=ALU.add,
                                                op1=ALU.mult))
                    v.wait_ge(sig_ready, c * 2 + y + 1)
                    v.tensor_tensor(act[:, y], sw_t, sw_s[:, y], ALU.mult).then_inc(act_ready, 1)

                def turn_out(y):
                    v.wait_ge(act_tr, c * 2 + y + 1)
                    v.tensor_copy(actT[:, y], ps[:, 3 + y, 0:256].rearrange("p (q s) -> p q s", q=2))\
                        .then_inc(actT_ready, 1)

                glu(0)
                v.wait_ge(sel_ps, c + 3)
                v.wait_ge(gathered, c * 16 + 32)
                indices(step, bass.ds(c + 2, 1))
                step(v.tensor_scalar(flatk, flatk, float(SLOTS), None, ALU.subtract))
                pick()
                turn_out(0)
                glu(1)
                turn_out(1)
                v.wait_ge(scattered, c * 16 + 16)
                v.wait_ge(idx_ready, c + 1)
                v.tensor_copy(idxs_c, row_all[:, bass.ds(c, 1)])
                step(v.tensor_copy(gate_c, gate_all[:, bass.ds(c, 1)]))
                v.wait_ge(dn_b, c + 1)
                v.tensor_scalar(ybuf, ps[:, 5, :], gate_c, None, ALU.mult).then_inc(y_ready, 1)
            assert n_in[0] == PER
            tail = [0]

            def tstep(ins):
                tail[0] += 1
                ins.then_inc(tail_chain, 1)
                v.wait_ge(tail_chain, tail[0])

            for i in range(NT):
                v.wait_ge(fin_in[i], 16)
                ins = v.tensor_tensor(ygain_f[:, i, :], yfin[:, i, :], gbf, ALU.mult)
            tstep(ins)
            v.wait_ge(sumsq, SQ_BEFORE[NORM_F] + 4)
            v.tensor_scalar(fin[:, 4:8], fin[:, 0:4], 1.0 / D, EPS, ALU.mult, ALU.add).then_inc(ms_ready, 1)
            v.wait_ge(root_ready, NORM_F + 1)
            r, t, ms = fin[:, 8:12], fin[:, 12:16], fin[:, 4:8]
            tstep(v.reciprocal(r, fin[:, 8:12]))
            tstep(v.tensor_tensor(t, r, r, ALU.mult))
            tstep(v.tensor_tensor(t, t, ms, ALU.mult))
            tstep(v.tensor_scalar(t, t, -0.5, 1.5, ALU.mult, ALU.add))
            tstep(v.tensor_tensor(r, r, t, ALU.mult))
            v.wait_ge(x2_back, 16)
            for i in range(NT):
                v.scalar_tensor_tensor(out=yfin[:, i, :], in0=ygain_f[:, i, :], scalar=r[:, i:i + 1],
                                       in1=x2fin[:, i, :], op0=ALU.mult, op1=ALU.add).then_inc(fin_ready, 1)

        @block.tensor
        def _(pe):
            pe.wait_ge(consts_in, 16)
            pe.wait_ge(vec_in, 16 * 8)
            pe.transpose(ps[:, 7, 0:88], vr, ident[0:88, 0:88])
            pe.transpose(ps[:, 7, 128:144], cposr, ident[0:16, 0:16]).then_inc(vt_ps, 1)
            pe.wait_ge(silu_ready, 1)

            def arrived(item):
                n = at_ring[item]
                pe.wait_ge(ring_in[RING[n][1]], 16 * (len(before_in_slot(n)) + 1))
                return ring_view(n)

            def ada(n):
                w = arrived(("ada", n))
                if n:
                    pe.wait_ge(row_sb, n)
                for j in range(KT):
                    g = j % 4
                    ins = pe.matmul(ps[32 * g:32 * g + 32, 2, :], silu_c[:, j, :], w[:, j, :],
                                    start=(j < 4), stop=(j >= 4))
                ins.then_inc(ada_ps, 1)

            def ada_t(n):
                pe.wait_ge(row_sb, n + 1)
                for q in range(4):
                    ins = pe.matmul(ps[:, 3, 4 * n + q:4 * n + q + 1], mrow[:, n % 2, q * P:(q + 1) * P],
                                    cf[:, C_SEL4:C_SEL4 + 1], start=True, stop=True)
                ins.then_inc(modc_ps, 1)

            for n in range(4):
                ada(n)
                if n:
                    ada_t(n - 1)
            ada_t(3)

            def turn_tiles(base, src, ready, count):
                for kt in range(KT):
                    if kt >= 4:
                        pe.wait_ge((ev_dve, ev_act)[kt % 2], (base + kt - 4) // 2 + 1)
                    for i in range(NT):
                        if kt == 0:
                            pe.wait_ge(ready, count(i))
                        ins = pe.transpose(ps[:, kt % 4, i * P:(i + 1) * P], src[:, i, kt * P:(kt + 1) * P], ident)
                    ins.then_inc(tile_tr, 1)

            pe.wait_ge(modc_sb, 1)
            turn_tiles(TILE_H, xn, xn_ready, lambda i: i + 1)
            pe.wait_ge(ev_dve, 4)
            pe.wait_ge(ev_act, 4)

            def project(n, between):
                w = arrived(("in", n))
                width = IN_COLS[n][1] - IN_COLS[n][0]
                for i in range(NT):
                    t = PJ[n] + i
                    if t >= 2:
                        pe.wait_ge(pj_ev, t - 1)
                    for kt in range(KT):
                        ins = pe.matmul(ps[:, t % 2, 0:width], hT[:, kt, i * P:(i + 1) * P], w[:, kt, :],
                                        start=(kt == 0), stop=(kt == KT - 1))
                    ins.then_inc(pj_ps, 1)
                    if i in between:
                        between[i]()

            def with_ada(n):
                def second():
                    ada_t(n)
                    ada(n + 1)
                return {0: lambda: ada(n), 1: second, 2: lambda: ada_t(n + 1)}

            def turn_group(g):
                kind, j = GROUPS[g]
                if g >= 4:
                    pe.wait_ge(tg_ev, g - 3)
                for i in range(NT):
                    if kind == "dup":
                        src = kdup[:, i, j].rearrange("p u d -> p (u d)")
                    else:
                        buf = stage[{"qraw": 0, "qrot": 0, "kwin": 1, "qdil": 0, "kdil": 1}[kind]]
                        src = buf[:, i, j * P:(j + 1) * P]
                    ins = pe.transpose(ps[:, 4 + g % 4, i * P:(i + 1) * P], src, ident)
                ins.then_inc(tg_ps, 1)

            def turn_groups(lo, hi):
                for g in range(lo, hi):
                    turn_group(g)

            def gain_product(n, bank_free):
                pe.wait_ge(diag_ready, n + 1)
                pe.wait_ge(*bank_free)
                for q in range(4):
                    ins = pe.matmul(ps[:, 2, q * P:(q + 1) * P], ones_f, diag[:, q, :], start=True, stop=True)
                ins.then_inc(diag_ps, 1)

            def hidden():
                gain_product(1, (gb_sb, 1))
                wk = arrived(("c1", 0))
                pe.wait_ge(wv_in, 32)
                pe.wait_ge(blk_ready, 1)
                pe.wait_ge(modc_sb, 2)
                for m in range(16):
                    pe.matmul(ps[0:64, 3, 0:256], blk[:, m, 0:2, :], wk[:, m, :], start=(m == 0), stop=(m == 15))
                    ins = pe.matmul(ps[64:128, 3, 0:256], blk[:, m, 2:4, :], wv_half[m // 8][:, m % 8, :],
                                    start=(m == 0), stop=(m == 15))
                ins.then_inc(hid_u, 1)

            def hidden_turned():
                pe.wait_ge(hid_ready, 1)
                pe.wait_ge(gb_sb, 2)
                for j in range(2):
                    ins = pe.transpose(ps[:, 2, j * P:(j + 1) * P], gel_u[:, j * P:(j + 1) * P], ident)
                ins.then_inc(hid_tr, 1)

            def compressed():
                pe.wait_ge(hid_sb, 1)
                pe.wait_ge(w2_in, 48)
                for j in range(2):
                    pe.matmul(ps[:, 3, 0:64], w2k[:, j].rearrange("p u d -> p (u d)"), hidT[:, j, 0:64],
                              start=(j == 0), stop=(j == 1))
                for g in range(2):
                    for j in range(2):
                        ins = pe.matmul(ps[:, 3, 64 + g * HD:64 + (g + 1) * HD],
                                        hidv[:, j, g].rearrange("p r c -> p (r c)"), w2v[:, j, :],
                                        start=(j == 0), stop=(j == 1))
                ins.then_inc(cv_ps, 1)

            project(0, with_ada(4))
            project(1, with_ada(6))
            pe.wait_ge(pj_ev, PJ[0] + NT)
            turn_groups(0, 4)
            project(2, {})
            pe.wait_ge(roped, 1)
            turn_groups(4, 8)
            pe.wait_ge(roped, 2)
            turn_groups(8, 14)
            project(3, with_ada(8))
            pe.wait_ge(roped, 3)
            turn_groups(14, 16)
            project(4, with_ada(10))
            pe.wait_ge(roped, 4)
            turn_groups(16, 20)
            project(5, {0: lambda: gain_product(0, (row_sb, 12)), 1: hidden, 2: hidden_turned, 3: compressed})
            pe.wait_ge(roped, 5)
            turn_groups(20, 24)
            gain_product(2, (gb_sb, 2))
            pe.wait_ge(cv_sb, 1)
            pe.wait_ge(bconst, 7)
            pe.wait_ge(tg_ev, len(GROUPS))
            for i in range(NT):
                rhs = bc(cm_b[:, 32 * i:32 * (i + 1)], 1, 8)
                pe.matmul(ps[:, 4 + i // 2, (i % 2) * 256:(i % 2 + 1) * 256], identb, rhs, start=(i % 2 == 0),
                          stop=False, skip_group_check=True)
            for pair in range(4):
                for i in range(NT):
                    at = (i % 2) * 256 + pair * 64
                    ins = pe.matmul(ps[:, 4 + i // 2, at:at + 64], qraw[:, pair, i * P:(i + 1) * P],
                                    kcT[:, pair // 2].rearrange("p u c -> p (u c)"), start=False, stop=(pair == 3),
                                    skip_group_check=True)
                if pair == 1:
                    gain_product(3, (gb_sb, 3))
            ins.then_inc(sc_ps, 1)
            pe.wait_ge(gb_sb, 4)
            pe.wait_ge(pj_ev, 4 * 6)

            def qk(u):
                ty, pr, i = units[u]
                w = P * (i + 1)
                if u >= 2:
                    pe.wait_ge(exp_done, u - 1)
                b = u % 2 * 2
                for h in range(2):
                    rows = slice(HD * h, HD * h + HD)
                    q = (qdil[rows, pr - 4] if ty == N_DIL else qrot[rows, pr])[:, i * P:(i + 1) * P]
                    k = (kdil[rows, pr - 4] if ty == N_DIL else (kslc, kwin)[ty][rows, pr // 2])[:, 0:w]
                    pe.matmul(ps[:, b + h, 0:w], q, k, start=True, stop=False)
                for h in range(2):
                    if ty == N_DIL:
                        ins = pe.matmul(ps[:, b + h, 0:w], identb, mb_b[:, (3 - i) * P:512], start=False, stop=True)
                    else:
                        ins = pe.matmul(ps[:, b + h, i * P:w], identb, trib, start=False, stop=True)
                ins.then_inc(qk_done, 1)

            def copied(u):
                if u < DIL_U:
                    pe.wait_ge(pt_dve, u + 1)
                else:
                    pe.wait_ge(pt_act, u - DIL_U + 1)

            def turn(u):
                pe.wait_ge(scaled_pool, u + 1)
                pe.wait_ge(scaled_act, u + 1)
                if u >= 1:
                    copied(u - 1)
                for h in range(2):
                    for kb in range(units[u][2] + 1):
                        cols = slice(kb * P, (kb + 1) * P)
                        ins = pe.transpose(ps[:, 4 + h, cols], probs[:, u % 4, h, cols], ident)
                ins.then_inc(tr_done, 1)

            def turn_compressed(g):
                pe.wait_ge(pc_ready, 1)
                if g:
                    pe.wait_ge(pc_sb, g)
                for i in range(NT):
                    ins = pe.transpose(ps[:, 7, i * P:(i + 1) * P], p_cmp[:, i, g * P:(g + 1) * P], ident)
                ins.then_inc(pc_tr, 1)

            turns = [0]

            def pv(u):
                ty, pr, i = units[u]
                bank = 6 + pr % 2
                copied(u)
                if (u == 0 or u - 1 in pair_last) and pr >= 2:
                    pe.wait_ge(o_ev, pr - 1)
                    pe.wait_ge(o_sq, pr - 1)
                if ty == N_WIN and i == 0:
                    pe.wait_ge(pc_sb, 2)
                    for h in range(2):
                        r = 32 * (pr % 2 * 2 + h)
                        ins = pe.matmul(ps[64 * h:64 * h + 64, bank, :], vc4[r:r + 32, pr // 2, :],
                                        pcT[r:r + 32, pr // 2].rearrange("p i q -> p (i q)"), start=False, stop=False,
                                        skip_group_check=True)
                        ins.then_inc(row_turn, 1)
                        turns[0] += 1
                        pe.wait_ge(row_turn, turns[0])
                for kb in range(i + 1):
                    for h in range(2):
                        hd = 2 * pr + h
                        val = v_dil[:, kb, (hd - 8) * HD:(hd - 7) * HD] if ty == N_DIL else \
                            (v_slc, v_win)[ty][:, kb, pr // 2 * HD:(pr // 2 + 1) * HD]
                        first = kb == 0 and (ty == N_DIL or ty == N_SLC and i == 0)
                        ins = pe.matmul(ps[64 * h:64 * h + 64, bank, i * P:(i + 1) * P], val,
                                        pT[:, u % 2, h, kb * P:(kb + 1) * P], start=first,
                                        stop=(ty != N_SLC and kb == i), skip_group_check=True)
                ins.then_inc(pv_done, 1)

            for u in range(3):
                qk(u)
            for u in range(UNITS):
                if u == 0:
                    pe.wait_ge(sc_in, 1)
                turn(u)
                if u:
                    pv(u - 1)
                if u in (1, 2):
                    turn_compressed(u - 1)
                if u + 3 < UNITS:
                    qk(u + 3)
            pv(UNITS - 1)

            def square_sums():
                pe.wait_ge(sq_added, 6)
                for grp in range(2):
                    for i in range(NT):
                        ins = pe.matmul(ps[:, 7, grp * 4 + i:grp * 4 + i + 1], osq[:, grp * 4, i * P:(i + 1) * P],
                                        ones_f[:, 0:1], start=True, stop=True)
                ins.then_inc(osum_ps, 1)

            pe.wait_ge(o_sq, 8)
            pe.wait_ge(o_ev, 8)
            for n in range(2):
                w = arrived(("wo", n))
                for grp in range(2):
                    for i in range(NT):
                        if n:
                            pe.wait_ge((y_nsa, y_sum)[grp], i + 1)
                        elif grp == 0 and i == 2:
                            square_sums()
                        elif grp and i == 3:
                            pe.wait_ge(orstd_ready, 1)
                        for j in range(4):
                            kt = grp * 4 + j
                            ins = pe.matmul(ps[:, 4 * grp + i, :], oT[:, kt, i * P:(i + 1) * P], w[:, kt, :],
                                            start=(j == 0), stop=(j == 3))
                        ins.then_inc(wo_ps, 1)
            pe.wait_ge(x2_ready, NT)
            turn_tiles(TILE_2, xn2, xn_ready, lambda i: NT + i + 1)
            pe.wait_ge(ev_dve, 8)
            pe.wait_ge(ev_act, 8)
            pe.wait_ge(wr_in, 16)
            for i in range(NT):
                for kt in range(KT):
                    ins = pe.matmul(ps[:, 4, 32 * i:32 * (i + 1)], hT[:, kt, i * P:(i + 1) * P], wr[:, kt, :],
                                    start=(kt == 0), stop=(kt == KT - 1))
            ins.then_inc(logit_ps, 1)
            pe.wait_ge(mask_ready, 1)
            for i in range(NT):
                for j in range(i + 1):
                    pe.matmul(ps[:, 5, 32 * i:32 * (i + 1)], usb if j == i else onesb, maskb[:, j, :],
                              start=(j == 0), stop=(j == i))
            for i in range(NT):
                ins = pe.matmul(ps[:, 6, 0:32], onesb, maskb[:, i, :], start=(i == 0), stop=(i == NT - 1))
            ins.then_inc(count_ps, 1)

            def pick_sum():
                for n in range(16):
                    ins = pe.matmul(ps[:, 6, 0:6], sel[:, n, :], rt[:, n, :], start=(n == 0), stop=(n == 15))
                ins.then_inc(sel_ps, 1)

            def turn_rows():
                for q in range(4):
                    ins = pe.transpose(ps[:, 2, q * P:(q + 1) * P], xg[:, q * P:(q + 1) * P], ident)
                ins.then_inc(xg_tr, 1)

            for m in range(2):
                pe.wait_ge(sel_ready, m + 1)
                if m:
                    pe.wait_ge(idx_ready, m)
                pick_sum()
            pe.wait_ge(moved, 1)
            turn_rows()
            pe.wait_ge(ctab_ready, 1)
            with pe.Fori(0, N_EXP // 2) as e2:
                for par in range(2):
                    chunks = pe.value_load(ctab[0:1, bass.ds(e2 * 2 + par, 1)], min_val=1, max_val=8)
                    first = pe.value_load(ctab[0:1, bass.ds(e2 * 2 + (par + 32), 1)], min_val=0, max_val=64)
                    weights_here = e2 * 16 + 16
                    with pe.Fori(0, chunks) as j:
                        c = first + j
                        pe.wait_ge(sel_ready, c + 3)
                        pe.wait_ge(idx_ready, c + 2)
                        pick_sum()
                        pe.wait_ge(xgT_ready, c + 1)
                        pe.wait_ge(biasw_in[par], weights_here)

                        def turn_act(y):
                            pe.wait_ge(act_ready, c * 2 + y + 1)
                            for q in range(2):
                                ins = pe.transpose(ps[:, 3 + y, q * P:(q + 1) * P], act[:, y, q * P:(q + 1) * P], ident)
                            ins.then_inc(act_tr, 1)

                        for y in range(2):
                            pe.wait_ge((a_in, b_in)[y][par], weights_here * 2)
                            for h in range(2):
                                col = 1024 * h + 512 * y
                                pe.matmul(ps[64 * h:64 * h + 64, y, :], onesb[0:3, 0:SLOTS],
                                          biasw[:, par, col:col + 512], start=True, stop=False)
                            for kt in range(KT):
                                if y == 1 and kt == 5:
                                    turn_act(0)
                                for h in range(2):
                                    ins = pe.matmul(ps[64 * h:64 * h + 64, y, :], xgT[:, kt, :],
                                                    upw[par][y][:, kt, h, :], start=False, stop=(kt == KT - 1))
                            ins.then_inc((up_a, up_b)[y], 1)
                        for h in range(2):
                            pe.matmul(ps[64 * h:64 * h + 64, 5, :], onesb[0:3, 0:SLOTS],
                                      biasw[:, par, 2048 + 512 * h:2560 + 512 * h], start=True, stop=False)
                        for y in range(2):
                            pe.wait_ge(actT_ready, c * 2 + y + 1)
                            pe.wait_ge(d_in[y], (e2 * 2 + par) * 32 + 32)
                            for q in range(2):
                                if y == 0 and q == 1:
                                    turn_act(1)
                                for s in range(2):
                                    for h in range(2):
                                        last = y == 1 and q == 1 and s == 1
                                        ins = pe.matmul(ps[64 * h:64 * h + 64, 5, :],
                                                        actT[:, y, q, s * SLOTS:(s + 1) * SLOTS],
                                                        dnw[:, y, s, q, 512 * h:512 * (h + 1)],
                                                        start=False, stop=last)
                            ins.then_inc((dn_a, dn_b)[y], 1)
                            if y == 0:
                                pe.wait_ge(moved, c + 2)
                                turn_rows()


_INS = ["x", "c", "positions", "w_ada", "b_ada", "g_pre_mix", "g_post_mix", "g_pre_ffn", "g_post_ffn", "w_in",
        "cmp_pos", "w_cmp_k1", "w_cmp_k2", "w_cmp_v1", "w_cmp_v2", "g_out_nsa", "g_out_dil", "w_o", "w_router",
        "b_router", "w_up", "b_up", "w_down", "b_down"]


def kernel(**inputs):
    import concourse.bacc as _bacc
    from concourse.bass_utils import run_bass_kernel_spmd as _run

    nc = _bacc.Bacc("TRN2", target_bir_lowering=False, num_devices=1)
    arrays, args = {}, {}
    for name in _INS:
        arr = np.ascontiguousarray(inputs[name])
        arrays[f"in_{name}"] = arr
        args[name] = nc.dram_tensor(f"in_{name}", arr.shape, mybir.dt.from_np(arr.dtype), kind="ExternalInput").ap()
    out = nc.dram_tensor("out_y", (SEQ, D), F32, kind="ExternalOutput").ap()
    hybrid_layer(nc, args, out)
    r = _run(nc, [arrays], core_ids=[0])
    return np.asarray(r.results[0]["out_y"]).reshape(1, SEQ, D)
```
